# Optimizing a Trainium2 kernel written in Bass

```python
import jax, jax.numpy as jnp
from jax import lax
import numpy as np

D_MODEL = 1024
BATCH = 1
SEQ = 1024
DEPTH = 2
DEC_BATCH = 8
DEC_SEQ = 1
PAST_LEN = 8192
PAGE_SIZE = 128

N_EVEN = (DEPTH + 1) // 2
N_ODD = DEPTH // 2
HG_H = 4
HG_DK = 128
HG_DV = D_MODEL // 2 // HG_H
NSA_H = 8
NSA_DH = D_MODEL // 2 // NSA_H
NSA_KV = 2
NSA_R = NSA_H // NSA_KV
NSA_BLK = 64
NSA_TOPK = 16
NSA_WINDOW = 512
NSA_CMP_HID = NSA_DH
NSA_QB = 128
NSA_Q = NSA_H * NSA_DH
GLA_H = 4
GLA_DK = D_MODEL // 2 // GLA_H
GLA_DV = D_MODEL // GLA_H
GLA_RANK = 16
GLA_TAU = 16.0
CHUNK = 32
D_FF = ((-(-8 * D_MODEL // 3) + 255) // 256) * 256
EPS = 1e-6
NEG = -1e30
TINY = 1e-30

HG_W = 2 * HG_H * HG_DK + 2 * HG_H * HG_DV
NSA_W = NSA_Q + 6 * NSA_KV * NSA_DH + 3 * NSA_H
EVEN_W = HG_W + NSA_W
EVEN_OUT = HG_H * HG_DV + NSA_H * NSA_DH
ODD_W = 2 * GLA_H * GLA_DK + 2 * GLA_H * GLA_DV + GLA_RANK
ODD_OUT = GLA_H * GLA_DV

kernel_name = 'hybrid_hgrn2_nsa_gla_decoder_step'

def rmsnorm(x, g):
    xf = x.astype(jnp.float32)
    y = xf * lax.rsqrt(jnp.mean(xf * xf, axis=-1, keepdims=True) + EPS)
    return (y * g.astype(jnp.float32)).astype(x.dtype)

def masked_softmax(s, mask, axes):
    s = jnp.where(mask, s, NEG)
    m = jnp.max(s, axis=axes, keepdims=True)
    p = jnp.where(mask, jnp.exp(s - m), 0.0)
    return p / jnp.maximum(jnp.sum(p, axis=axes, keepdims=True), TINY)

def alibi_slopes(n):
    return jnp.asarray(2.0 ** (-8.0 * np.arange(1, n + 1) / n), dtype=jnp.float32)

def chunk_gla(q, k, v, logf, s0):
    B, T, H, K = q.shape
    V = v.shape[-1]
    C = min(CHUNK, T)
    n = -(-T // C)
    pad = n * C - T

    def prep(a):
        a = jnp.pad(a.astype(jnp.float32), ((0, 0), (0, pad), (0, 0), (0, 0)))
        return a.reshape(B, n, C, H, a.shape[-1]).transpose(1, 0, 2, 3, 4)

    qc, kc, vc, gc = prep(q), prep(k), prep(v), prep(logf)
    causal = jnp.tril(jnp.ones((C, C), bool))[None, :, :, None, None]

    def step(S, inp):
        qi, ki, vi, gi = inp
        b = jnp.cumsum(gi, axis=1)
        dec = jnp.exp(jnp.where(causal, b[:, :, None] - b[:, None, :], -jnp.inf))
        a = jnp.einsum('bthk,bshk,btshk->bhts', qi, ki, dec)
        o = jnp.einsum('bthk,bhkv->bthv', qi * jnp.exp(b), S) + jnp.einsum('bhts,bshv->bthv', a, vi)
        bl = b[:, -1]
        S = jnp.exp(bl)[..., None] * S + jnp.einsum('bshk,bshv->bhkv', ki * jnp.exp(bl[:, None] - b), vi)
        return S, o

    S, o = lax.scan(step, s0.astype(jnp.float32), (qc, kc, vc, gc))
    o = o.transpose(1, 0, 2, 3, 4).reshape(B, n * C, H, V)[:, :T]
    return o, S

def hgrn2_mixer(p, lb, gain, s0):
    B, T, _ = p.shape
    hk, hv = HG_H * HG_DK, HG_H * HG_DV
    q = jax.nn.silu(p[..., :hk].astype(jnp.float32)).reshape(B, T, HG_H, HG_DK)
    f = lb + (1.0 - lb) * jax.nn.sigmoid(p[..., hk:2 * hk].astype(jnp.float32))
    f = f.reshape(B, T, HG_H, HG_DK)
    i = p[..., 2 * hk:2 * hk + hv].reshape(B, T, HG_H, HG_DV)
    og = p[..., 2 * hk + hv:].reshape(B, T, HG_H, HG_DV)
    o, S = chunk_gla(q, 1.0 - f, i, jnp.log(f), s0)
    o = rmsnorm(o, gain) * jax.nn.sigmoid(og.astype(jnp.float32))
    return o.reshape(B, T, hv), S

def gla_mixer(p, wa2, ba, gain, s0):
    B, T, _ = p.shape
    hk, hv = GLA_H * GLA_DK, GLA_H * GLA_DV
    q = p[..., :hk].reshape(B, T, GLA_H, GLA_DK) * (GLA_DK ** -0.5)
    k = p[..., hk:2 * hk].reshape(B, T, GLA_H, GLA_DK)
    v = p[..., 2 * hk:2 * hk + hv].reshape(B, T, GLA_H, GLA_DV)
    a1 = p[..., 2 * hk + hv:2 * hk + hv + GLA_RANK]
    r = p[..., 2 * hk + hv + GLA_RANK:].reshape(B, T, GLA_H, GLA_DV)
    logf = (jax.nn.log_sigmoid((a1 @ wa2 + ba).astype(jnp.float32)) / GLA_TAU).reshape(B, T, GLA_H, GLA_DK)
    o, S = chunk_gla(q, k, v, logf, s0)
    o = rmsnorm(o, gain) * jax.nn.silu(r.astype(jnp.float32))
    return o.reshape(B, T, hv), S

def compress_blocks(x, pe, w1, w2):
    B, n, l, G, dh = x.shape
    z = (x + pe[:, None, :]).transpose(0, 1, 3, 2, 4).reshape(B, n, G, l * dh)
    return jax.nn.silu(z @ w1) @ w2

def nsa_mixer(p, pos0, past_kv, win_buf, cmp_pos, cmp_w1, cmp_w2):
    B, T, _ = p.shape
    G, R, dh = NSA_KV, NSA_R, NSA_DH
    q = p[..., :NSA_Q].reshape(B, T, G, R, dh)
    kv_new = p[..., NSA_Q:NSA_Q + 6 * G * dh].reshape(B, T, 6, G, dh)
    gates = jax.nn.sigmoid(p[..., NSA_Q + 6 * G * dh:].astype(jnp.float32)).reshape(B, T, G, R, 3)
    rows = kv_new[:, :, :4]
    win_new = kv_new[:, :, 4:]
    L = pos0 + T
    nblk = -(-L // NSA_BLK)
    parts = [] if past_kv is None else [past_kv.astype(rows.dtype)]
    parts = parts + [rows, jnp.zeros((B, nblk * NSA_BLK - L, 4, G, dh), rows.dtype)]
    blocks = jnp.concatenate(parts, axis=1).reshape(B, nblk, NSA_BLK, 4, G, dh)
    slopes = alibi_slopes(NSA_H).reshape(G, R)
    scale = dh ** -0.5
    qpos = pos0 + jnp.arange(T)

    kc = compress_blocks(blocks[:, :, :, 0], cmp_pos[0], cmp_w1[0], cmp_w2[0])
    vc = compress_blocks(blocks[:, :, :, 1], cmp_pos[1], cmp_w1[1], cmp_w2[1])
    blk = jnp.arange(nblk)
    dist_c = (qpos[:, None] - (blk * NSA_BLK + NSA_BLK - 1)[None, :]).astype(jnp.float32)
    s_c = jnp.einsum('btgrd,bngd->bgrtn', q, kc).astype(jnp.float32) * scale - slopes[:, :, None, None] * dist_c
    p_c = masked_softmax(s_c, dist_c >= 0, (-1,))
    o_cmp = jnp.einsum('bgrtn,bngd->btgrd', p_c, vc.astype(jnp.float32))

    imp = jnp.sum(p_c, axis=2)
    forced = (blk[None, :] == (qpos // NSA_BLK)[:, None]) | (blk[None, :] == 0)
    started = blk[None, :] * NSA_BLK <= qpos[:, None]
    score = jnp.where(forced, jnp.inf, jnp.where(started, imp, -jnp.inf))
    ksel = min(NSA_TOPK, nblk)
    _, idx = lax.top_k(score, ksel)

    ks = blocks[:, :, :, 2].transpose(0, 3, 1, 2, 4)
    vs = blocks[:, :, :, 3].transpose(0, 3, 1, 2, 4)
    qb_len = NSA_QB if T % NSA_QB == 0 else T
    nqb = T // qb_len
    qx = q.reshape(B * nqb, qb_len, G, R, dh)
    ix = idx.reshape(B, G, nqb, qb_len, ksel).transpose(0, 2, 1, 3, 4).reshape(B * nqb, G, qb_len, ksel)
    flat = jnp.arange(B * nqb)
    garr = jnp.arange(G)[:, None, None]

    def sel_body(args):
        b, i, qb, ib = args
        kg = ks[b][garr, ib]
        vg = vs[b][garr, ib]
        pq = pos0 + i * qb_len + jnp.arange(qb_len)
        kpos = ib[..., None] * NSA_BLK + jnp.arange(NSA_BLK)
        dist = (pq[None, :, None, None] - kpos).astype(jnp.float32)
        ss = jnp.einsum('qgrd,gqkld->grqkl', qb, kg).astype(jnp.float32) * scale - slopes[:, :, None, None, None] * dist[:, None]
        pp = masked_softmax(ss, (dist >= 0)[:, None], (-2, -1))
        return jnp.einsum('grqkl,gqkld->qgrd', pp, vg.astype(jnp.float32))

    o_slc = lax.map(sel_body, (flat // nqb, flat % nqb, qx, ix)).reshape(B, T, G, R, dh)

    if win_buf is None:
        wk, lbuf = win_new, 0
    else:
        wk, lbuf = jnp.concatenate([win_buf.astype(win_new.dtype), win_new], axis=1), win_buf.shape[1]
    new_win = wk[:, wk.shape[1] - min(NSA_WINDOW, L):]
    wkp = jnp.pad(wk, ((0, 0), (NSA_WINDOW - lbuf, 0), (0, 0), (0, 0), (0, 0)))
    span = NSA_WINDOW + qb_len
    qw = q.reshape(B, nqb, qb_len, G, R, dh).transpose(1, 0, 2, 3, 4, 5)

    def win_body(args):
        i, qb = args
        kv = lax.dynamic_slice_in_dim(wkp, i * qb_len, span, axis=1)
        pq = pos0 + i * qb_len + jnp.arange(qb_len)
        pk = pos0 - NSA_WINDOW + i * qb_len + jnp.arange(span)
        dist = pq[:, None] - pk[None, :]
        mask = (dist >= 0) & (dist < NSA_WINDOW) & (pk[None, :] >= 0)
        ss = jnp.einsum('bqgrd,bkgd->bgrqk', qb, kv[:, :, 0]).astype(jnp.float32) * scale - slopes[:, :, None, None] * dist.astype(jnp.float32)
        pp = masked_softmax(ss, mask, (-1,))
        return jnp.einsum('bgrqk,bkgd->bqgrd', pp, kv[:, :, 1].astype(jnp.float32))

    o_win = lax.map(win_body, (jnp.arange(nqb), qw)).transpose(1, 0, 2, 3, 4, 5).reshape(B, T, G, R, dh)

    o = gates[..., 0:1] * o_cmp + gates[..., 1:2] * o_slc + gates[..., 2:3] * o_win
    return o.reshape(B, T, NSA_H * dh), rows, new_win

def forward(x, pos0, pool, page_table, win_bufs, hg_states, gla_states, W):
    B, T, _ = x.shape
    lb_all = jnp.cumsum(jax.nn.softmax(W['hg_lb_logits'].astype(jnp.float32), axis=0), axis=0)
    rows_out, win_out, hg_out, gla_out = [], [], [], []
    for l in range(DEPTH):
        i = l // 2
        xn = rmsnorm(x, W['norm_mix'][l])
        if l % 2 == 0:
            if pool is None:
                past, wbuf = None, None
                s0 = jnp.zeros((B, HG_H, HG_DK, HG_DV), jnp.float32)
            else:
                past = pool[i, page_table].reshape(B, -1, 4, NSA_KV, NSA_DH)
                wbuf, s0 = win_bufs[i], hg_states[i]
            p = xn @ W['w_in_even'][i]
            o_h, S = hgrn2_mixer(p[..., :HG_W], lb_all[i], W['hg_norm'][i], s0)
            o_n, rows, new_win = nsa_mixer(p[..., HG_W:], pos0, past, wbuf,
                                           W['nsa_cmp_pos'][i], W['nsa_cmp_w1'][i], W['nsa_cmp_w2'][i])
            mix = jnp.concatenate([o_h.astype(x.dtype), o_n.astype(x.dtype)], axis=-1) @ W['w_out_even'][i]
            rows_out.append(rows)
            win_out.append(new_win)
            hg_out.append(S)
        else:
            s0 = jnp.zeros((B, GLA_H, GLA_DK, GLA_DV), jnp.float32) if gla_states is None else gla_states[i]
            p = xn @ W['w_in_odd'][i]
            o_g, S = gla_mixer(p, W['gla_wa2'][i], W['gla_ba'][i], W['gla_norm'][i], s0)
            mix = o_g.astype(x.dtype) @ W['w_out_odd'][i]
            gla_out.append(S)
        x = x + mix.astype(x.dtype)
        h = rmsnorm(x, W['norm_ffn'][l])
        gu = h @ W['ffn_w13'][l]
        x = x + ((jax.nn.silu(gu[..., :D_FF]) * gu[..., D_FF:]) @ W['ffn_w2'][l]).astype(x.dtype)
    y = rmsnorm(x, W['norm_final'])
    return y, jnp.stack(rows_out), jnp.stack(win_out), jnp.stack(hg_out), jnp.stack(gla_out)

def setup_inputs(seed: int = 0) -> dict:
    key = jax.random.key(seed)
    ks = jax.random.split(key, 24)
    n_pages = PAST_LEN // PAGE_SIZE
    n_used = DEC_BATCH * n_pages
    n_pool = n_used + max(1, n_used // 4)
    win_len = min(NSA_WINDOW, PAST_LEN)

    def nrm(k, shape, s):
        return s * jax.random.normal(k, shape, jnp.float32)

    page_table = jax.random.permutation(ks[6], n_pool)[:n_used].reshape(DEC_BATCH, n_pages).astype(jnp.int32)
    return {
        'x_prompt': nrm(ks[0], (BATCH, SEQ, D_MODEL), 1.0),
        'x_sample': nrm(ks[1], (DEC_BATCH, DEC_SEQ, D_MODEL), 1.0),
        'cache_nsa_kv': nrm(ks[2], (N_EVEN, n_pool, PAGE_SIZE, 4, NSA_KV, NSA_DH), 1.0),
        'cache_win_kv': nrm(ks[3], (N_EVEN, DEC_BATCH, win_len, 2, NSA_KV, NSA_DH), 1.0),
        'state_hgrn': nrm(ks[4], (N_EVEN, DEC_BATCH, HG_H, HG_DK, HG_DV), 0.5),
        'state_gla': nrm(ks[5], (N_ODD, DEC_BATCH, GLA_H, GLA_DK, GLA_DV), 0.5),
        'page_table': page_table,
        'w_in_even': nrm(ks[7], (N_EVEN, D_MODEL, EVEN_W), D_MODEL ** -0.5),
        'hg_lb_logits': nrm(ks[8], (N_EVEN + 1, HG_H * HG_DK), 0.5),
        'hg_norm': 1.0 + nrm(ks[9], (N_EVEN, HG_DV), 0.02),
        'nsa_cmp_pos': nrm(ks[10], (N_EVEN, 2, NSA_BLK, NSA_DH), 0.1),
        'nsa_cmp_w1': nrm(ks[11], (N_EVEN, 2, NSA_BLK * NSA_DH, NSA_CMP_HID), (NSA_BLK * NSA_DH) ** -0.5),
        'nsa_cmp_w2': nrm(ks[12], (N_EVEN, 2, NSA_CMP_HID, NSA_DH), NSA_CMP_HID ** -0.5),
        'w_out_even': nrm(ks[13], (N_EVEN, EVEN_OUT, D_MODEL), EVEN_OUT ** -0.5),
        'w_in_odd': nrm(ks[14], (N_ODD, D_MODEL, ODD_W), D_MODEL ** -0.5),
        'gla_wa2': nrm(ks[15], (N_ODD, GLA_RANK, GLA_H * GLA_DK), GLA_RANK ** -0.5),
        'gla_ba': nrm(ks[16], (N_ODD, GLA_H * GLA_DK), 0.1),
        'gla_norm': 1.0 + nrm(ks[17], (N_ODD, GLA_DV), 0.02),
        'w_out_odd': nrm(ks[18], (N_ODD, ODD_OUT, D_MODEL), ODD_OUT ** -0.5),
        'norm_mix': 1.0 + nrm(ks[19], (DEPTH, D_MODEL), 0.02),
        'norm_ffn': 1.0 + nrm(ks[20], (DEPTH, D_MODEL), 0.02),
        'norm_final': 1.0 + nrm(ks[21], (D_MODEL,), 0.02),
        'ffn_w13': nrm(ks[22], (DEPTH, D_MODEL, 2 * D_FF), D_MODEL ** -0.5),
        'ffn_w2': nrm(ks[23], (DEPTH, D_FF, D_MODEL), D_FF ** -0.5),
    }

def reference(x_prompt, x_sample, cache_nsa_kv, cache_win_kv, state_hgrn, state_gla, page_table,
              w_in_even, hg_lb_logits, hg_norm, nsa_cmp_pos, nsa_cmp_w1, nsa_cmp_w2, w_out_even,
              w_in_odd, gla_wa2, gla_ba, gla_norm, w_out_odd, norm_mix, norm_ffn, norm_final,
              ffn_w13, ffn_w2):
    W = dict(w_in_even=w_in_even, hg_lb_logits=hg_lb_logits, hg_norm=hg_norm, nsa_cmp_pos=nsa_cmp_pos,
             nsa_cmp_w1=nsa_cmp_w1, nsa_cmp_w2=nsa_cmp_w2, w_out_even=w_out_even, w_in_odd=w_in_odd,
             gla_wa2=gla_wa2, gla_ba=gla_ba, gla_norm=gla_norm, w_out_odd=w_out_odd, norm_mix=norm_mix,
             norm_ffn=norm_ffn, norm_final=norm_final, ffn_w13=ffn_w13, ffn_w2=ffn_w2)
    past_len = page_table.shape[1] * cache_nsa_kv.shape[2]
    y_prompt, kv_p, win_p, hg_p, gla_p = forward(x_prompt, 0, None, None, None, None, None, W)
    y_sample, kv_s, win_s, hg_s, gla_s = forward(x_sample, past_len, cache_nsa_kv, page_table,
                                                 cache_win_kv, state_hgrn, state_gla, W)
    return (y_prompt, y_sample, kv_p, kv_s, win_p, win_s, hg_p, hg_s, gla_p, gla_s)


_drawn_inputs = setup_inputs


def setup_inputs(seed=0):
    import zlib

    import numpy as np

    out = dict(_drawn_inputs(seed))
    spreads = {}
    factors = {'hg_norm': 4.737, 'gla_norm': 22.627, 'norm_final': 7.395, 'norm_ffn': 3.727}
    for name, (base, spread) in spreads.items():
        noise = np.random.default_rng([zlib.crc32(name.encode()), seed]).standard_normal(out[name].shape)
        drawn = base * np.exp(spread * noise) if base else spread * noise
        out[name] = __import__('jax').numpy.asarray(drawn.astype(out[name].dtype))
    for name, factor in factors.items():
        out[name] = (out[name] * factor).astype(out[name].dtype)
    return out
```

```python
from contextlib import ExitStack, contextmanager

import numpy as np

import concourse.bass as bass
from concourse import mybir

F32 = mybir.dt.float32
F32R = mybir.dt.float32r
I32 = mybir.dt.int32
ALU = mybir.AluOpType
ACT = mybir.ActivationFunctionType
AX_X = mybir.AxisListType.X
ds = bass.ds

P = 128
DM = 1024
KT = DM // P
SEQ = 1024
NB = 8
TOK = SEQ + NB
CH = TOK // 3
CHUNKS = [(c, slice(c * CH, (c + 1) * CH)) for c in range(3)]
QT = SEQ // P
PAST = 8192
PAGE = 128
NPG = PAST // PAGE
G, R, DH = 2, 4, 64
ROWS = NB * G * R
BLK = 64
PBLK = SEQ // BLK
SBLK = PAST // BLK
TOPK = 16
WIN = 512
FF = 2816
FT = FF // P
FH = FT // 2
GT = TOK // 2
GC = GT // 2
EPS = 1e-6
NEG = -1e30
TINY = 1e-30
HEADS = 4
GV = 256
RANK = 16
TAU = 16.0
LEVELS = 7

TQ, TKC, TVC, TKS, TVS, TKW, TVW, TGATE, NNSA = 0, 4, 5, 6, 7, 8, 9, 10, 11


class Tally:

    def __init__(self, sem):
        self.sem, self.n, self.reg, self.start, self.per = sem, 0, None, 0, 0

    def enter(self, reg, per):
        self.reg, self.start, self.per = reg, self.n, per

    def leave(self, times):
        assert self.n - self.start == self.per, (self.n - self.start, self.per)
        self.n, self.reg = self.start + times * self.per, None

    def now(self):
        return self.n if self.reg is None else self.reg * self.per + self.n

    def up(self, ins, by=1):
        ins.then_inc(self.sem, by)
        self.n += by

    def chain(self, eng, ins):
        self.up(ins)
        eng.wait_ge(self.sem, self.now())


class Memory:
    pass


ONE = 1


@contextmanager
def started(nc, sems):
    for sem in sems:
        nc.gpsimd.sem_inc(sem, ONE)
    nc.all_engine_barrier()
    with nc.Block() as block:
        yield block


@contextmanager
def phase(nc, label):
    sems = []

    def sem(name):
        sems.append(nc.alloc_semaphore(f"{label}_{name}"))
        return sems[-1]

    with ExitStack() as ctx:
        yield ctx, sem, sems
    nc.clear_and_free_semaphores(sems)
    nc.all_engine_barrier()


def carve(t, off, shape, p0=0, p1=P):
    n = int(np.prod(shape))
    v = t[p0:p1, off:off + n]
    if len(shape) == 1:
        return v
    names = "abcde"[:len(shape)]
    return v.rearrange(f"p ({' '.join(names)}) -> p {' '.join(names)}", **dict(zip(names, shape)))


def alloc(nc, ctx, m):
    def sb(name, shape, dt=F32):
        return ctx.enter_context(nc.sbuf_tensor(name, shape, dt))

    m.XT = sb("XT", [P, KT, TOK])
    m.ident = sb("ident", [P, P])
    m.ones = sb("ones", [P, P])
    m.eye8 = sb("eye8", [P, NB, NB])
    m.gains = sb("gains", [P, 5, KT])
    m.LB = sb("LB", [P, 2, HEADS])
    m.keep = sb("keep", [P, 336])
    m.cum = sb("cum", [P, LEVELS + 2, P])
    m.lmask = sb("lmask", [P, LEVELS + 1, P])
    m.PS = ctx.enter_context(nc.psum_tensor("PS", [P, 8, 512], F32))
    m.w_in = [ctx.enter_context(nc.semaphore(f"w_in{i}")) for i in range(2)]
    m.acc_ready = [ctx.enter_context(nc.semaphore(f"acc_ready{i}")) for i in range(3)]
    m.acc_free = [ctx.enter_context(nc.semaphore(f"acc_free{i}")) for i in range(3)]
    m.w_cmp_in = ctx.enter_context(nc.semaphore("w_cmp_in"))
    m.pool = Tally(ctx.enter_context(nc.semaphore("pool_step")))
    m.act = Tally(ctx.enter_context(nc.semaphore("act_step")))
    m.dve = Tally(ctx.enter_context(nc.semaphore("dve_step")))
    m.t = 2


@contextmanager
def mixer_memory(nc, m, label):
    with ExitStack() as ctx:
        def sb(name, shape):
            return ctx.enter_context(nc.sbuf_tensor(f"{label}_{name}", shape, F32))

        m.XN = sb("XN", [P, KT, TOK])
        m.WR = sb("WR", [P, 2, FT * P])
        m.AR = sb("AR", [P, 19914])
        m.NT = carve(m.AR, 0, (NNSA, TOK))
        yield


@contextmanager
def output_memory(nc, m, label):
    with nc.sbuf_tensor(f"{label}_OT", [P, KT * TOK], F32) as m.OT:
        m.O = carve(m.OT, 0, (KT, TOK))
        yield


def load_tile(sp, m, off, src, kt, i=0, per=0):
    t = m.t + off
    sp.wait_ge(m.acc_ready[2], i * per + t - 1)
    sp.dma_start(m.WR[:, t % 2, 0:kt * P], src).then_inc(m.w_in[t % 2], 16)


def mm_tile(pe, m, off, kt, rhs, i=0, per=0):
    t = m.t + off
    pe.wait_ge(m.w_in[t % 2], i * (per // 2 * 16) + 16 * (t // 2 + 1))
    for c, cols in CHUNKS:
        pe.wait_ge(m.acc_free[c], i * per + t)
        for k in range(kt):
            mm = pe.matmul(m.PS[:, c, 0:CH], m.WR[:, t % 2, k * P:(k + 1) * P], rhs[:, k, cols],
                           start=(k == 0), stop=(k == kt - 1))
        mm.then_inc(m.acc_ready[c], 1)


def evac_wait(eng, m, off, i=0, per=0):
    for c in range(3):
        eng.wait_ge(m.acc_free[c], i * per + m.t + off + 1)


def acc_wait(eng, m, off, c, i=0, per=0):
    eng.wait_ge(m.acc_ready[c], i * per + m.t + off + 1)


def load_stream(nc, m, d, sp, x_in):
    for n in range(KT // 2):
        sp.dma_start(m.XT[:, 2 * n:2 * n + 2], d["xT"][:, 2 * n:2 * n + 2]).then_inc(x_in[n], 16)
    sp.dma_start(m.gains[:], d["gains"]).then_inc(x_in[KT // 2 - 1], 16)


def fill_constants(m, pool):
    c = m.pool

    def select(view, op, base, pattern, mult, fill=0.0):
        c.chain(pool, pool.affine_select(out=view, in_=view, compare_op=op, fill=fill, base=base,
                                         pattern=pattern, channel_multiplier=mult))

    c.up(pool.memset(m.ones[:], 1.0))
    c.up(pool.memset(m.ident[:], 0.0))
    c.up(pool.memset(m.eye8[:], 0.0))
    c.up(pool.memset(m.cum[:], 1.0))
    c.chain(pool, pool.memset(m.lmask[:], 1.0))
    select(m.ident[:], ALU.not_equal, 0, [[-1, P]], 1, 1.0)
    select(m.eye8[:], ALU.not_equal, 0, [[1, NB], [-1, NB]], 0, 1.0)
    select(m.cum[:, 0, :], ALU.is_ge, 0, [[1, P]], -1)
    select(m.cum[:, LEVELS + 1, :], ALU.is_ge, -1, [[-1, P]], 1)
    for lv in range(LEVELS):
        h = P >> (lv + 1)
        n = P // (2 * h)
        half = m.cum[:, 1 + lv, :].rearrange("p (b c h) -> p b c h", b=n, c=2)
        select(half[:, :, 1, :], ALU.is_ge, -h, [[-2 * h, n], [0, h]], 1)
        select(half[:, :, 1, :], ALU.is_ge, h, [[2 * h, n], [1, h]], -1)
        select(half[:, :, 0, :], ALU.is_ge, -1, [[-2 * h, n], [-1, h]], 1)
        select(half[:, :, 0, :], ALU.is_ge, h - 1, [[2 * h, n], [0, h]], -1)
        pair = m.lmask[:, lv, :].rearrange("p (b c h) -> p b c h", b=n, c=2)
        select(pair[:, :, 1, :], ALU.is_ge, 0, [[-2 * h, n], [0, h]], 1)
        select(pair[:, :, 1, :], ALU.is_ge, h - 1, [[2 * h, n], [0, h]], -1)
        c.chain(pool, pool.memset(pair[:, :, 0, :], 0.0))
    select(m.lmask[:, LEVELS, :], ALU.is_equal, 0, [[-1, P]], 1)


def norm_roots(nc, m, SQ, RSTD, d=None):
    with (nc.semaphore("sq_ready") as sq_ready, nc.semaphore("sq_added") as sq_added,
          nc.semaphore("ss_ready") as ss_ready, nc.semaphore("std_ready") as std_ready, ExitStack() as ctx):
        x_in = [ctx.enter_context(nc.semaphore(f"x_in{n}")) for n in range(KT // 2)] if d else []
        block = ctx.enter_context(nc.Block())
        ones_set = m.pool.n + 1
        if d:
            @block.sync
            def _(sp):
                load_stream(nc, m, d, sp, x_in)
                sp.wait_ge(x_in[KT // 2 - 1], 32)

            @block.gpsimd
            def _(pool):
                fill_constants(m, pool)

        @block.scalar
        def _(act):
            for k in range(KT):
                if d and k % 2 == 0:
                    act.wait_ge(x_in[k // 2], 16 if k // 2 < KT // 2 - 1 else 32)
                if k >= 2:
                    act.wait_ge(sq_added, k - 1)
                act.activation(SQ[:, k % 2], m.XT[:, k], ACT.Square).then_inc(sq_ready, 1)
            for c, cols in CHUNKS:
                act.wait_ge(ss_ready, c + 1)
                act.activation(RSTD[:, cols], m.PS[:, 5 + c, 0:CH], ACT.Sqrt, bias=EPS, scale=1.0 / DM)\
                   .then_inc(std_ready, 1)

        @block.vector
        def _(dve):
            for k in range(KT):
                dve.wait_ge(sq_ready, k + 1)
                if k == 0:
                    dve.tensor_copy(RSTD, SQ[:, 0]).then_inc(sq_added, 1)
                else:
                    dve.wait_ge(sq_added, k)
                    dve.tensor_tensor(RSTD, RSTD, SQ[:, k % 2], ALU.add).then_inc(sq_added, 1)
            for c, cols in CHUNKS:
                dve.wait_ge(std_ready, c + 1)
                m.dve.chain(dve, dve.reciprocal(RSTD[:, cols], RSTD[:, cols]))

        @block.tensor
        def _(pe):
            if d:
                for slot in range(2):
                    pe.sem_inc(m.w_in[slot], 16)
                for c in range(3):
                    pe.sem_inc(m.acc_ready[c], 2)
                    pe.sem_inc(m.acc_free[c], 2)
                pe.wait_ge(m.pool.sem, ones_set)
            pe.wait_ge(sq_added, KT)
            for c, cols in CHUNKS:
                pe.matmul(m.PS[:, 5 + c, 0:CH], m.ones[:], RSTD[:, cols], start=True, stop=True)\
                  .then_inc(ss_ready, 1)


def norm(nc, m, gi, d=None):
    RSTD = carve(m.AR, 2 * TOK, (TOK,))
    norm_roots(nc, m, carve(m.AR, 0, (2, TOK)), RSTD, d)
    with nc.Block() as block:
        @block.vector
        def _(dve):
            for k in range(KT):
                m.dve.up(dve.scalar_tensor_tensor(out=m.XN[:, k], in0=m.XT[:, k], scalar=m.gains[:, gi, k:k + 1],
                                                  in1=RSTD, op0=ALU.mult, op1=ALU.mult))


def add_projection(nc, m, label, w):
    HEAD = ONE + 5
    with ExitStack() as mem, phase(nc, label) as (ctx, sem, sems):
        def sb(name, shape, dt):
            return mem.enter_context(nc.sbuf_tensor(f"{label}_{name}", shape, dt))

        XH, XL = sb("XH", [P, KT, TOK], F32R), sb("XL", [P, KT, TOK], F32R)
        RAW = sb("RAW", [P, 2, KT * P], F32)
        WH, WL = sb("WH", [P, 2, KT * P], F32R), sb("WL", [P, 2, KT * P], F32R)
        raw_in = [sem(f"raw_in{i}") for i in range(2)]
        wh_ready, wl_ready = sem("wh_ready"), sem("wl_ready")
        xh_ready, xl_ready = sem("xh_ready"), sem("xl_ready")
        sum_ready = sem("sum_ready")
        added = sem("added")
        block = ctx.enter_context(started(nc, sems + 5 * [wl_ready, sum_ready, added]))

        @block.sync
        def _(sp):
            with sp.Fori(0, KT // 2) as i:
                for u in range(2):
                    sp.wait_ge(wl_ready, i * 2 + u - 1 + HEAD)
                    sp.dma_start(RAW[:, u], w[ds(i * 2 + u, 1)]).then_inc(raw_in[u], 16)

        @block.gpsimd
        def _(pool):
            with pool.Fori(0, KT // 2) as i:
                for u in range(2):
                    pool.wait_ge(wh_ready, i * 2 + u + 1 + ONE)
                    pool.tensor_tensor(WL[:, u], RAW[:, u], WH[:, u].bitcast(F32), ALU.subtract).then_inc(wl_ready, 1)

        @block.scalar
        def _(act):
            def upper(i):
                for u in range(2):
                    act.wait_ge(raw_in[u], i * 16 + 16 + ONE)
                    act.wait_ge(sum_ready, i * 6 + u * 3 - 3 + HEAD)
                    act.activation(WH[:, u], RAW[:, u], ACT.Copy).then_inc(wh_ready, 1)

            for c, cols in CHUNKS:
                act.activation(XH[:, :, cols], m.O[:, :, cols], ACT.Copy).then_inc(xh_ready, 1)
                if c == 0:
                    upper(0)
            with act.Fori(0, KT // 2 - 1) as i:
                upper(i + 1)

        @block.tensor
        def _(pe):
            with pe.Fori(0, KT // 2) as i:
                for u in range(2):
                    pe.wait_ge(wl_ready, i * 2 + u + 1 + HEAD)
                    for c, cols in CHUNKS:
                        pe.wait_ge(xl_ready, c + 1 + ONE)
                        pe.wait_ge(added, i * 6 + u * 3 + c - 5 + HEAD)
                        for k in range(KT):
                            for n, (wgt, x) in enumerate(((WH, XH), (WH, XL), (WL, XH))):
                                mm = pe.matmul(m.PS[:, u * 3 + c, 0:CH], wgt[:, u, k * P:(k + 1) * P], x[:, k, cols],
                                               start=(k + n == 0), stop=(k == KT - 1 and n == 2))
                        mm.then_inc(sum_ready, 1)

        @block.vector
        def _(dve):
            for c, cols in CHUNKS:
                dve.wait_ge(xh_ready, c + 1 + ONE)
                dve.tensor_tensor(XL[:, :, cols], m.O[:, :, cols], XH[:, :, cols].bitcast(F32), ALU.subtract)\
                   .then_inc(xl_ready, 1)
            with dve.Fori(0, KT // 2) as i:
                for u in range(2):
                    for c, cols in CHUNKS:
                        dve.wait_ge(sum_ready, i * 6 + u * 3 + c + 1 + HEAD)
                        x = m.XT[:, ds(i * 2 + u, 1), cols]
                        dve.tensor_tensor(x, m.PS[:, u * 3 + c:u * 3 + c + 1, 0:CH], x, ALU.add).then_inc(added, 1)


def ffn(nc, m, gi, w13, w2):
    T1, T2 = 2 * FT, 2 * KT
    F1, F2 = 2 * FT, KT
    HEAD = ONE + 3
    with ExitStack() as mem, phase(nc, f"ffn{gi}") as (ctx, sem, sems):
        def sb(name, shape, dt):
            return mem.enter_context(nc.sbuf_tensor(f"ffn{gi}_{name}", shape, dt))

        XH, XL = sb("XH", [P, KT, GT], F32R), sb("XL", [P, KT, GT], F32R)
        HH, HL = sb("HH", [P, FT, GT], F32R), sb("HL", [P, FT, GT], F32R)
        RAW = sb("RAW", [P, 2, FH * P], F32)
        WH, WL = sb("WH", [P, 2, FH * P], F32R), sb("WL", [P, 2, FH * P], F32R)
        SIL, TMP = sb("SIL", [P, 2, GC], F32), sb("TMP", [P, 2, GC], F32)
        RSTD = sb("RSTD", [P, TOK], F32)
        norm_roots(nc, m, RAW[:].rearrange("p a b -> p (a b)")[:, 0:2 * TOK].rearrange("p (a b) -> p a b", a=2),
                   RSTD[:])

        raw_in = [sem(f"raw_in{i}") for i in range(2)]
        wh_ready, wl_ready = sem("wh_ready"), sem("wl_ready")
        x_ready, xh_ready, xl_ready = sem("x_ready"), sem("xh_ready"), sem("xl_ready")
        first_ready = sem("first_ready")
        w_used = sem("w_used")
        silu_ready, h_ready = sem("silu_ready"), sem("h_ready")
        added = sem("added")
        hh_ready, hl_ready = sem("hh_ready"), sem("hl_ready")
        block = ctx.enter_context(started(nc, sems + 3 * [wl_ready, w_used, silu_ready, h_ready, hl_ready, added]))

        def loads(g, stage):
            return g * (T1 + T2) + stage * T1

        def sums(g, stage):
            return g * (F1 + F2) + stage * F1

        @block.sync
        def _(sp):
            def load(t0, i, u, src, kt):
                t = t0 + u
                sp.wait_ge(wl_ready, i * 2 + t - 1 + HEAD)
                sp.dma_start(RAW[:, t % 2, 0:kt * P], src).then_inc(raw_in[t % 2], 16)

            for g in range(2):
                with sp.Fori(0, FT) as i:
                    for u in range(2):
                        load(loads(g, 0), i, u, w13[ds(i * 2 + u, 1)], KT)
                with sp.Fori(0, KT) as i:
                    for u in range(2):
                        load(loads(g, 1), i, u, w2[ds(i, 1), :, u * FH * P:(u + 1) * FH * P], FH)

        @block.gpsimd
        def _(pool):
            def rest(t0, i, u, kt):
                t = t0 + u
                raw, hi, lo = (w[:, t % 2, 0:kt * P] for w in (RAW, WH, WL))
                pool.wait_ge(wh_ready, i * 2 + t + 1 + ONE)
                pool.tensor_tensor(lo, raw, hi.bitcast(F32), ALU.subtract).then_inc(wl_ready, 1)

            for g in range(2):
                with pool.Fori(0, FT) as i:
                    for u in range(2):
                        rest(loads(g, 0), i, u, KT)
                with pool.Fori(0, KT) as i:
                    for u in range(2):
                        rest(loads(g, 1), i, u, FH)

        @block.tensor
        def _(pe):
            def passes(t, f, c, kt, hi, lo, k0=0, last=None):
                cols = slice(c * GC, (c + 1) * GC)
                for k in range(kt):
                    w = slice(k * P, (k + 1) * P)
                    for n, (wgt, act) in enumerate(((WH, hi), (WH, lo), (WL, hi))):
                        mm = pe.matmul(m.PS[:, f % 2 * 2 + c, 0:GC], wgt[:, t % 2, w], act[:, k0 + k, cols],
                                       start=(k0 + k + n == 0),
                                       stop=(n == 2 and k == kt - 1 and last is not False))
                return mm

            for g in range(2):
                pe.wait_ge(xl_ready, (g + 1) * KT + ONE)
                pe.wait_ge(added, g * 2 * F2 + HEAD)
                with pe.Fori(0, FT) as i:
                    for u in range(2):
                        t, f = loads(g, 0) + u, sums(g, 0) + u
                        pe.wait_ge(wl_ready, i * 2 + t + 1 + HEAD)
                        for c in range(2):
                            pe.wait_ge((silu_ready, h_ready)[u], i * 2 + g * F1 + c - 1 + HEAD)
                            passes(t, f, c, KT, XH, XL).then_inc((first_ready, w_used)[c], 1)
                pe.wait_ge(hl_ready, (g + 1) * F1 + HEAD)
                with pe.Fori(0, KT // 2) as i:
                    for v in range(2):
                        f = sums(g, 1) + v
                        for u in range(2):
                            t = loads(g, 1) + v * 2 + u
                            pe.wait_ge(wl_ready, i * 4 + t + 1 + HEAD)
                            for c in range(2):
                                if u == 0:
                                    pe.wait_ge(added, i * 4 + (g * F2 + v) * 2 + c - 3 + HEAD)
                                mm = passes(t, f, c, FH, HH, HL, u * FH, u == 1)
                                if c == 1:
                                    mm.then_inc(w_used, 1)
                                elif u == 1:
                                    mm.then_inc(first_ready, 1)

        @block.scalar
        def _(act):
            def upper(t0, i, kt):
                for u in range(2):
                    t = t0 + u
                    act.wait_ge(raw_in[t % 2], i * 16 + (t // 2 + 1) * 16 + ONE)
                    act.wait_ge(w_used, i * 2 + t - 1 + HEAD)
                    act.activation(WH[:, t % 2, 0:kt * P], RAW[:, t % 2, 0:kt * P], ACT.Copy).then_inc(wh_ready, 1)

            def upper_tokens(g):
                for k in range(KT):
                    act.wait_ge(x_ready, g * KT + k + 1 + ONE)
                    buf = (TMP, SIL)[k % 2][:].rearrange("p a b -> p (a b)")
                    act.activation(XH[:, k], buf, ACT.Copy).then_inc(xh_ready, 1)

            def hidden(g, i, following):
                for c in range(2):
                    if c == 0:
                        act.wait_ge(first_ready, i * 2 + sums(g, 0) + 1 + ONE)
                    else:
                        act.wait_ge(w_used, i * 2 + loads(g, 0) + 1 + HEAD)
                    act.wait_ge(h_ready, i * 2 + g * F1 + c - 1 + HEAD)
                    act.activation(SIL[:, c], m.PS[:, c, 0:GC], ACT.Silu).then_inc(silu_ready, 1)
                upper(*following)
                for c in range(2):
                    act.wait_ge(h_ready, i * 2 + g * F1 + c + 1 + HEAD)
                    act.activation(HH[:, ds(i, 1), c * GC:(c + 1) * GC], TMP[:, c:c + 1], ACT.Copy)\
                       .then_inc(hh_ready, 1)

            upper(loads(0, 0), 0, KT)
            upper_tokens(0)
            for g in range(2):
                with act.Fori(0, FT - 1) as i:
                    hidden(g, i, (loads(g, 0) + 2, i, KT))
                hidden(g, FT - 1, (loads(g, 1), 0, FH))
                if g == 0:
                    upper_tokens(1)
                with act.Fori(0, KT - 1) as i:
                    upper(loads(g, 1) + 2, i, FH)
                if g == 0:
                    upper(loads(1, 0), 0, KT)

        @block.vector
        def _(dve):
            def norm_tokens(g):
                if g == 1:
                    dve.wait_ge(w_used, loads(0, 1) + HEAD)
                    dve.wait_ge(hl_ready, F1 + HEAD)
                tokens = slice(g * GT, (g + 1) * GT)
                for k in range(KT + 1):
                    if k < KT:
                        if k >= 2:
                            dve.wait_ge(xl_ready, g * KT + k - 1 + ONE)
                        dve.scalar_tensor_tensor(out=(TMP, SIL)[k % 2][:].rearrange("p a b -> p (a b)"),
                                                 in0=m.XT[:, k, tokens], scalar=m.gains[:, gi, k:k + 1],
                                                 in1=RSTD[:, tokens], op0=ALU.mult, op1=ALU.mult).then_inc(x_ready, 1)
                    if k >= 1:
                        dve.wait_ge(xh_ready, g * KT + k + ONE)
                        dve.tensor_tensor(XL[:, k - 1], (TMP, SIL)[(k - 1) % 2][:].rearrange("p a b -> p (a b)"),
                                          XH[:, k - 1].bitcast(F32), ALU.subtract).then_inc(xl_ready, 1)

            norm_tokens(0)
            for g in range(2):
                with dve.Fori(0, FT) as i:
                    t, f = loads(g, 0) + 1, sums(g, 0) + 1
                    for c in range(2):
                        if c == 0:
                            dve.wait_ge(first_ready, i * 2 + f + 1 + ONE)
                        else:
                            dve.wait_ge(w_used, i * 2 + t + 1 + HEAD)
                        dve.wait_ge(silu_ready, i * 2 + g * F1 + c + 1 + HEAD)
                        dve.wait_ge(hl_ready, i * 2 + g * F1 + c - 1 + HEAD)
                        dve.tensor_tensor(TMP[:, c], m.PS[:, 2 + c, 0:GC], SIL[:, c], ALU.mult).then_inc(h_ready, 1)
                    for c in range(2):
                        dve.wait_ge(hh_ready, i * 2 + g * F1 + c + 1 + ONE)
                        h = (slice(None), ds(i, 1), slice(c * GC, (c + 1) * GC))
                        dve.tensor_tensor(HL[h], TMP[:, c:c + 1], HH[h].bitcast(F32), ALU.subtract)\
                           .then_inc(hl_ready, 1)
                if g == 0:
                    norm_tokens(1)
                with dve.Fori(0, KT // 2) as i:
                    for v in range(2):
                        t, f = loads(g, 1) + 2 * v + 1, sums(g, 1) + v
                        for c in range(2):
                            if c == 0:
                                dve.wait_ge(first_ready, i * 2 + f + 1 + ONE)
                            else:
                                dve.wait_ge(w_used, i * 4 + t + 1 + HEAD)
                            x = m.XT[:, ds(i * 2 + v, 1), g * GT + c * GC:g * GT + (c + 1) * GC]
                            dve.tensor_tensor(x, m.PS[:, f % 2 * 2 + c:f % 2 * 2 + c + 1, 0:GC], x, ALU.add)\
                               .then_inc(added, 1)


def project_attention(nc, m, d):
    NT = m.NT
    with nc.Block() as block:
        @block.sync
        def _(sp):
            with sp.Fori(0, NNSA // 2) as i:
                for u in range(2):
                    load_tile(sp, m, u, d["w_even"][ds(i * 2 + u, 1)], KT, i, 2)
            load_tile(sp, m, TGATE, d["w_even"][TGATE], KT)
            for g in range(G):
                half = slice(g * DH, (g + 1) * DH)
                sp.dma_start(m.W1D[half], d["w1_dlh"]).then_inc(m.w_cmp_in, 16)
                sp.dma_start(m.W2D[half], d["w2_hd"]).then_inc(m.w_cmp_in, 16)
                sp.dma_start(m.PET[half], d["pe_dl"]).then_inc(m.w_cmp_in, 16)
            sp.dma_start(m.NSL, d["nslope"]).then_inc(m.w_cmp_in, 16)

        @block.tensor
        def _(pe):
            with pe.Fori(0, NNSA // 2) as i:
                for u in range(2):
                    mm_tile(pe, m, u, KT, m.XN, i, 2)
            mm_tile(pe, m, TGATE, KT, m.XN)

        @block.vector
        def _(dve):
            m.dve.up(dve.memset(m.VCB, 0.0))
            m.dve.chain(dve, dve.memset(m.KCZ, 0.0))

        @block.scalar
        def _(act):
            with act.Fori(0, 2) as i:
                for u in range(2):
                    for c, cols in CHUNKS:
                        acc_wait(act, m, u, c, i, 2)
                        act.activation(NT[:, ds(i * 2 + u, 1), cols], m.PS[:, c:c + 1, 0:CH], ACT.Copy,
                                       scale=DH ** -0.5).then_inc(m.acc_free[c], 1)
            with act.Fori(0, 3) as i:
                for u in range(2):
                    for c, cols in CHUNKS:
                        acc_wait(act, m, TKC + u, c, i, 2)
                        act.activation(NT[:, ds(i * 2 + (TKC + u), 1), cols], m.PS[:, c:c + 1, 0:CH], ACT.Copy)\
                           .then_inc(m.acc_free[c], 1)
            for c, cols in CHUNKS:
                acc_wait(act, m, TGATE, c)
                act.activation(NT[:, TGATE, cols], m.PS[:, c, 0:CH], ACT.Sigmoid).then_inc(m.acc_free[c], 1)
    m.t += NNSA


def store(nc, m, d):
    with nc.semaphore("y_out") as y_out, nc.Block() as block:
        @block.sync
        def _(sp):
            sp.dma_start(d["yT"], m.XN[:]).then_inc(y_out, 16)
            sp.wait_ge(y_out, 16)


def lower_bounds(nc, m, d):
    t = m.dve
    LG = carve(m.AR, 0, (2, HEADS))
    MX = carve(m.AR, 2 * HEADS, (HEADS,))
    with nc.semaphore("logits_in") as logits_in, nc.semaphore("exp_ready") as exp_ready, nc.Block() as block:
        @block.sync
        def _(sp):
            sp.dma_start(LG, d["lb"]).then_inc(logits_in, 16)

        @block.vector
        def _(dve):
            dve.wait_ge(logits_in, 16)
            t.chain(dve, dve.tensor_tensor(MX, LG[:, 0], LG[:, 1], ALU.max))
            t.chain(dve, dve.tensor_tensor(LG, LG, MX.unsqueeze(1).to_broadcast([P, 2, HEADS]), ALU.subtract))
            dve.wait_ge(exp_ready, 1)
            t.chain(dve, dve.tensor_tensor(MX, LG[:, 0], LG[:, 1], ALU.add))
            t.chain(dve, dve.reciprocal(MX, MX))
            t.chain(dve, dve.tensor_tensor(m.LB[:, 0], LG[:, 0], MX, ALU.mult))
            t.up(dve.tensor_scalar(m.LB[:, 1], m.LB[:, 0], -1.0, 1.0, ALU.mult, ALU.add))

        after = t.n - 4

        @block.scalar
        def _(act):
            act.wait_ge(t.sem, after)
            act.activation(LG, LG, ACT.Exp).then_inc(exp_ready, 1)


def gate_factor(nc, m, d):
    with nc.Block() as block:
        @block.sync
        def _(sp):
            load_tile(sp, m, 0, d["w_odd"][0], KT)

        @block.gpsimd
        def _(pool):
            m.pool.up(pool.memset(m.O[0:32, KT - 1, :], 1.0))

        @block.tensor
        def _(pe):
            mm_tile(pe, m, 0, KT, m.XN)

        ones_set = m.pool.n

        @block.scalar
        def _(act):
            act.wait_ge(m.pool.sem, ones_set)
            for c, cols in CHUNKS:
                acc_wait(act, m, 0, c)
                act.activation(m.O[0:RANK, KT - 1, cols], m.PS[0:RANK, c, 0:CH], ACT.Copy).then_inc(m.acc_free[c], 1)
    m.t += 1


def linear_attention(nc, m, d, gla):
    V = GV if gla else P
    VT = V // P
    NTL = 2 + 2 * VT
    w = d["w_odd"] if gla else d["w_even"]
    woff = 1 if gla else NNSA
    states_in, states_out, state_p = (d["gla_in"], d["gla_s"], d["gla_p"]) if gla else (d["hg_in"], d["hg_s"], d["hg_p"])
    at = [0]

    def take(*shape):
        v = carve(m.AR, at[0], shape)
        at[0] += int(np.prod(shape))
        assert at[0] <= m.AR.shape[1], (at[0], m.AR.shape)
        return v

    qT, kT, fT = take(TOK), take(TOK), None if gla else take(TOK)
    vT, gT = take(VT, TOK), take(VT, TOK)
    LN = take(QT, P)
    VN = take(QT, V)
    ON = take(QT + 1, V)
    EX = take(LEVELS + 2, P)
    QS, KS = take(2, LEVELS + 1, P), take(2, LEVELS + 1, P)
    AM = take(LEVELS + 1, P)
    AS = take(2, P)
    KN = take(2, P)
    S = take(2, V)
    DEC = take(QT)
    GN = take(VT)
    SSQ = take(QT + 1)
    FS = take(NB)
    QM = take(NB, NB)
    X0, X1 = m.WR[:, 0, KT * P:], m.WR[:, 1, KT * P:]
    NBG = 1024 // V
    NG = NB // NBG
    S0 = X0[:, 0:1024].rearrange("p (b v) -> p b v", b=NBG)
    WA = X0[0:RANK + 1, 1024:1024 + HEADS * P]
    KM = X1[0:NB, 0:NB * P].rearrange("p (b k) -> p b k", b=NB)
    KS8 = X1[0:NB, NB * P:(NB + 1) * P]
    VS = X1[0:NB, (NB + 1) * P:(NB + 1) * P + V]
    WAH = X1[0:RANK + 1, (NB + 3) * P:(NB + 4) * P]
    A1 = m.O[0:RANK + 1, KT - 1, :]
    XF = EX.rearrange("p a b -> p (a b)")
    CF = m.cum[:].rearrange("p a b -> p (a b)")
    b_x, b_y = m.PS[:, 3:6].rearrange("p a b -> p (a b)"), m.PS[:, 6:8].rearrange("p a b -> p (a b)")
    NLN = 0 if gla else 2
    NNAT = NLN + 2 * VT

    with phase(nc, "gla" if gla else "hgrn") as (ctx, sem, sems):
        small_in = sem("small_in")
        kf_ready = sem("kf_ready")
        lf_ready = sem("lf_ready")
        fs_ready = sem("fs_ready")
        wah_ready = sem("wah_ready")
        z_ready = sem("z_ready")
        ls_step = sem("ls_step")
        ln_step = sem("ln_step")
        nat_ready = sem("nat_ready")
        nat_read = sem("nat_read")
        smp_turned = sem("smp_turned")
        smp_step = sem("smp_step")
        sums_ready = sem("sums_ready")
        ex_ready = sem("ex_ready")
        qs_ready = sem("qs_ready")
        ks_ready = sem("ks_ready")
        a_ready = sem("a_ready")
        am_ready = sem("am_ready")
        as_ready = sem("as_ready")
        kt_ready = sem("kt_ready")
        kn_ready = sem("kn_ready")
        u_ready = sem("u_ready")
        s_ready = sem("s_ready")
        o_ready = sem("o_ready")
        o_read = sem("o_read")
        st_in = sem("st_in")
        st_out = sem("st_out")
        outer_ready = sem("outer_ready")
        st_ready = sem("st_ready")
        st_used = sem("st_used")
        sq_ready = sem("sq_ready")
        on_step = sem("on_step")
        turn_ready = sem("turn_ready")
        turn_read = sem("turn_read")
        pst_out = sem("pst_out")
        block = ctx.enter_context(started(nc, sems))

        @block.sync
        def _(sp):
            if gla:
                sp.dma_start(WA, d["wa2"]).then_inc(small_in, 16)
            sp.dma_start(GN, d["gla_gain"] if gla else d["hg_gain"]).then_inc(small_in, 16)
            with sp.Fori(0, HEADS) as h:
                for u in range(NTL):
                    load_tile(sp, m, u, w[ds(h * NTL + (woff + u), 1)], KT, h, NTL)
            sp.wait_ge(st_out, HEADS * NG * 16 + ONE)
            sp.wait_ge(pst_out, HEADS * 16 + ONE)

        @block.gpsimd
        def _(pool):
            with pool.Fori(0, HEADS) as h:
                for c in range(QT):
                    pool.wait_ge(ex_ready, h * QT + c + 1 + ONE)
                    evac_wait(pool, m, 1, h, NTL)
                    if not gla:
                        pool.wait_ge(kf_ready, h * 2 + 2 + ONE)
                    pool.wait_ge(u_ready, h * QT + max(c - 1, 0) + ONE)
                    pool.tensor_tensor(KS[:, c % 2], EX[:, 1:LEVELS + 2],
                                       kT[:, c * P:(c + 1) * P].unsqueeze(1).to_broadcast([P, LEVELS + 1, P]),
                                       ALU.mult).then_inc(ks_ready, 1)

        @block.tensor
        def _(pe):
            def turn(out, in_):
                n = in_.shape[0]
                return pe.transpose(out, in_, m.ident[0:n, 0:n])

            def project(h):
                pe.wait_ge(o_read, h * (QT + 1) + ONE)
                pe.wait_ge(s_ready, h * (QT + 1) + ONE)
                for u in range(2 + VT):
                    mm_tile(pe, m, u, KT, m.XN, h, NTL)

            def recur(h):
                if gla:
                    pe.wait_ge(wah_ready, h + 1 + ONE)
                    for c in range(QT):
                        pe.matmul(b_x[:, c * P:(c + 1) * P], A1[:, c * P:(c + 1) * P], WAH, start=True, stop=True)
                    pe.matmul(b_x[:, SEQ:TOK], WAH, A1[:, SEQ:TOK], start=True, stop=True).then_inc(z_ready, 1)
                for u in range(2 + VT, NTL):
                    mm_tile(pe, m, u, KT, m.XN, h, NTL)
                pe.wait_ge(turn_read, h * 3 * VT + ONE)
                if not gla:
                    pe.wait_ge(lf_ready, h + 1 + ONE)
                for n in range(NNAT):
                    src = fT if n < NLN else vT[:, (n - NLN) // 2]
                    if n == NLN:
                        evac_wait(pe, m, 1 + VT, h, NTL)
                    if n >= 2:
                        pe.wait_ge(nat_read, h * NNAT + n - 1 + ONE)
                    for c in range(4):
                        j = n % 2 * 4 + c
                        mm = turn(m.PS[:, 6 + n % 2, c * P:(c + 1) * P], src[:, j * P:(j + 1) * P])
                    mm.then_inc(nat_ready, 1)
                evac_wait(pe, m, NTL - 1, h, NTL)
                if not gla:
                    pe.wait_ge(kf_ready, h * 2 + 2 + ONE)
                turn(m.PS[0:NB, 0, 0:P], kT[:, SEQ:TOK])
                for v in range(VT):
                    mm = turn(m.PS[0:NB, 0, (1 + v) * P:(2 + v) * P], vT[:, v, SEQ:TOK])
                mm.then_inc(smp_turned, 1)
                pe.wait_ge(nat_read, (h + 1) * NNAT + ONE)
                if gla:
                    pe.wait_ge(ln_step, h * 4 + 4 + ONE)
                pe.wait_ge(smp_step, h * 4 + 2 + ONE)

                def sums(c):
                    pe.wait_ge(ex_ready, h * QT + c + ONE)
                    for a, b in ((0, 512), (512, 1024), (1024, 1152)):
                        mm = pe.matmul(b_x[:, a:b], LN[:, c], CF[:, a:b], start=True, stop=True)
                    mm.then_inc(sums_ready, 1)

                def update(c):
                    pe.wait_ge(kn_ready, h * QT + c + 1 + ONE)
                    pe.wait_ge(s_ready, h * (QT + 1) + c + 1 + ONE)
                    pe.matmul(m.PS[:, 2, 0:V], KN[:, c % 2], VN[:, c], start=True, stop=True).then_inc(u_ready, 1)

                def outputs(c):
                    pe.wait_ge(as_ready, h * QT + c + 1 + ONE)
                    pe.wait_ge(s_ready, h * (QT + 1) + c + 1 + ONE)
                    pe.wait_ge(o_read, h * (QT + 1) + c + ONE)
                    pe.matmul(m.PS[:, 1, 0:V], QS[:, c % 2, 0], S[:, c % 2], start=True, stop=False)
                    pe.matmul(m.PS[:, 1, 0:V], AS[:, c % 2], VN[:, c], start=False, stop=True).then_inc(o_ready, 1)

                sums(0)
                for c in range(QT):
                    if c + 1 < QT:
                        sums(c + 1)
                    if c >= 1:
                        update(c - 1)
                        outputs(c - 1)
                    pe.wait_ge(qs_ready, (h * QT + c + 1) * 2 + ONE)
                    pe.wait_ge(ks_ready, h * QT + c + 1 + ONE)
                    pe.wait_ge(am_ready, h * QT + c + ONE)
                    for lv in range(LEVELS):
                        pe.matmul(b_y[:, lv * P:(lv + 1) * P], KS[:, c % 2, lv], QS[:, c % 2, 1 + lv],
                                  start=True, stop=True)
                    pe.matmul(b_y[:, LEVELS * P:], kT[:, c * P:(c + 1) * P], qT[:, c * P:(c + 1) * P],
                              start=True, stop=True).then_inc(a_ready, 1)
                    turn(m.PS[:, 0, 0:P], KS[:, c % 2, LEVELS]).then_inc(kt_ready, 1)
                update(QT - 1)
                outputs(QT - 1)

                pe.wait_ge(smp_step, h * 4 + 4 + ONE)
                for g in range(NG):
                    pe.wait_ge(st_ready, h * NB + g * NBG + ONE)
                    for b in range(NBG):
                        mm = pe.matmul(b_x[:, b * V:(b + 1) * V], KM[:, g * NBG + b], VS, start=True, stop=True)
                    mm.then_inc(outer_ready, 1)
                    pe.wait_ge(st_ready, h * NB + (g + 1) * NBG + ONE)
                    for b in range(NBG):
                        n = g * NBG + b
                        mm = pe.matmul(m.PS[0:NB, 5, 0:V], QM[:, n], S0[:, b], start=(n == 0), stop=(n == NB - 1))
                    mm.then_inc(st_used, 1)
            def turn_back(h):
                pe.wait_ge(on_step, h * 2 + 2 + ONE)
                for v in range(VT):
                    for b in range(3):
                        n = v * 3 + b
                        if n >= 2:
                            pe.wait_ge(turn_read, h * 3 * VT + n - 1 + ONE)
                        if b < 2:
                            for c in range(4):
                                mm = turn(m.PS[:, 6 + n % 2, c * P:(c + 1) * P], ON[:, b * 4 + c, v * P:(v + 1) * P])
                        else:
                            mm = turn(m.PS[:, 6 + n % 2, 0:P], ON[:, QT, v * P:(v + 1) * P])
                        mm.then_inc(turn_ready, 1)

            project(0)
            with pe.Fori(0, HEADS - 1) as h:
                recur(h)
                project(h + 1)
                turn_back(h)
            recur(HEADS - 1)
            turn_back(HEADS - 1)

        @block.scalar
        def _(act):
            def evac(off, dst, func, scale=1.0):
                for c, cols in CHUNKS:
                    acc_wait(act, m, off, c, h, NTL)
                    act.activation(dst[:, cols], m.PS[:, c, 0:CH], func, scale=scale).then_inc(m.acc_free[c], 1)

            if gla:
                act.wait_ge(small_in, 32 + ONE)
            with act.Fori(0, HEADS) as h:
                act.wait_ge(st_out, h * (NG * 16) + ONE)
                act.wait_ge(st_used, h * NG + ONE)
                act.dma_start(S0, states_in[ds(h, 1), 0]).then_inc(st_in, 16)
                if gla:
                    act.wait_ge(z_ready, h + ONE)
                    act.activation(WAH, WA[:, ds(h * P, P)], ACT.Copy).then_inc(wah_ready, 1)
                act.wait_ge(smp_step, h * 4 + ONE)
                evac(0, qT, ACT.Copy if gla else ACT.Silu, P ** -0.5 if gla else 1.0)
                evac(1, kT if gla else fT, ACT.Copy if gla else ACT.Sigmoid)
                for v in range(VT):
                    evac(2 + v, vT[:, v], ACT.Copy)
                if gla:
                    act.wait_ge(z_ready, h + 1 + ONE)
                    act.activation(XF[:, 0:TOK], b_x[:, 0:TOK], ACT.Abs).then_inc(ls_step, 1)
                    act.wait_ge(ls_step, h * 3 + 1 + ONE)
                    act.activation(XF[:, 0:TOK], XF[:, 0:TOK], ACT.Exp, scale=-1.0).then_inc(ls_step, 1)
                    act.wait_ge(ls_step, h * 3 + 2 + ONE)
                    act.activation(XF[:, 0:TOK], XF[:, 0:TOK], ACT.Ln, bias=1.0).then_inc(ls_step, 1)
                else:
                    act.wait_ge(kf_ready, h * 2 + 2 + ONE)
                    act.activation(FS, fT[:, SEQ:TOK], ACT.Copy).then_inc(fs_ready, 1)
                    act.activation(fT[:, 0:SEQ], fT[:, 0:SEQ], ACT.Ln).then_inc(lf_ready, 1)
                act.wait_ge(turn_read, h * 3 * VT + ONE)
                for v in range(VT):
                    evac(2 + VT + v, gT[:, v], ACT.Silu if gla else ACT.Sigmoid)
                for n in range(NNAT):
                    act.wait_ge(nat_ready, h * NNAT + n + 1 + ONE)
                    b, v = n % 2, (n - NLN) // 2
                    dst = LN[:, b * 4:(b + 1) * 4] if n < NLN else VN[:, b * 4:(b + 1) * 4, v * P:(v + 1) * P]
                    act.activation(dst, m.PS[:, 6 + b, :].rearrange("p (a b) -> p a b", a=4), ACT.Copy)\
                       .then_inc(nat_read, 1)
                if gla:
                    act.wait_ge(ln_step, h * 4 + 4 + ONE)
                    act.activation(FS, FS, ACT.Exp).then_inc(fs_ready, 1)

                def expo(c):
                    act.wait_ge(sums_ready, h * QT + c + 1 + ONE)
                    act.wait_ge(qs_ready, (h * QT + c) * 2 + ONE)
                    act.wait_ge(ks_ready, h * QT + c + ONE)
                    act.activation(XF, b_x[:, 0:(LEVELS + 2) * P], ACT.Exp).then_inc(ex_ready, 1)

                def out(c):
                    act.wait_ge(o_ready, h * QT + c + 1 + ONE)
                    act.activation(ON[:, c], m.PS[:, 1, 0:V], ACT.Copy).then_inc(o_read, 1)

                expo(0)
                for c in range(QT):
                    if c + 1 < QT:
                        expo(c + 1)
                    if c >= 1:
                        out(c - 1)
                    act.wait_ge(kt_ready, h * QT + c + 1 + ONE)
                    act.activation(KN[:, c % 2], m.PS[:, 0, 0:P], ACT.Copy).then_inc(kn_ready, 1)
                out(QT - 1)
                act.wait_ge(s_ready, (h + 1) * (QT + 1) + ONE)
                act.dma_start(state_p[ds(h, 1)], S[:, 0]).then_inc(pst_out, 16)
                for g in range(NG):
                    act.wait_ge(st_ready, h * NB + (g + 1) * NBG + ONE)
                    act.dma_start(states_out[ds(h, 1), g], S0).then_inc(st_out, 16)
                    if g + 1 < NG:
                        act.wait_ge(st_out, h * (NG * 16) + (g + 1) * 16 + ONE)
                        act.wait_ge(st_used, h * NG + g + 1 + ONE)
                        act.dma_start(S0, states_in[ds(h, 1), g + 1]).then_inc(st_in, 16)
                act.wait_ge(st_used, (h + 1) * NG + ONE)
                act.activation(ON[0:NB, QT], m.PS[0:NB, 5, 0:V], ACT.Copy).then_inc(o_read, 1)
                act.wait_ge(o_read, (h + 1) * (QT + 1) + ONE)
                for c in range(QT + 1):
                    n = P if c < QT else NB
                    act.activation(AM[0:n, 0:VT].rearrange("p a b -> p (a b)"), ON[0:n, c], ACT.Square,
                                   accum_out=SSQ[0:n, c:c + 1]).then_inc(sq_ready, 1)
                    act.wait_ge(sq_ready, h * (QT + 2) + c + 1 + ONE)
                act.activation(SSQ, SSQ, ACT.Sqrt, bias=EPS, scale=1.0 / V).then_inc(sq_ready, 1)

        @block.vector
        def _(dve):
            def bc(x, *shape):
                return x.to_broadcast([x.shape[0], *shape])

            m.dve.up(dve.memset(SSQ, 1.0))
            m.dve.chain(dve, dve.memset(ON[:, QT], 0.0))
            dve.wait_ge(small_in, (32 if gla else 16) + ONE)
            with dve.Fori(0, HEADS) as h:
                if gla:
                    dve.wait_ge(ls_step, h * 3 + 3 + ONE)
                    LF = LN.rearrange("p a b -> p (a b)")
                    dve.scalar_tensor_tensor(out=LF, in0=b_x[:, 0:SEQ], scalar=0.0, in1=XF[:, 0:SEQ],
                                             op0=ALU.min, op1=ALU.subtract).then_inc(ln_step, 1)
                    dve.scalar_tensor_tensor(out=FS, in0=b_x[:, SEQ:TOK], scalar=0.0, in1=XF[:, SEQ:TOK],
                                             op0=ALU.min, op1=ALU.subtract).then_inc(ln_step, 1)
                    dve.wait_ge(ln_step, h * 4 + 2 + ONE)
                    dve.tensor_scalar(LF, LF, 1.0 / TAU, None, ALU.mult).then_inc(ln_step, 1)
                    dve.tensor_scalar(FS, FS, 1.0 / TAU, None, ALU.mult).then_inc(ln_step, 1)
                else:
                    evac_wait(dve, m, 1, h, NTL)
                    dve.tensor_scalar(fT, fT, m.LB[:, 1, ds(h, 1)], m.LB[:, 0, ds(h, 1)], ALU.mult, ALU.add)\
                       .then_inc(kf_ready, 1)
                    dve.wait_ge(kf_ready, h * 2 + 1 + ONE)
                    dve.tensor_scalar(kT, fT, -1.0, 1.0, ALU.mult, ALU.add).then_inc(kf_ready, 1)
                dve.wait_ge(smp_turned, h + 1 + ONE)
                dve.tensor_copy(KS8, m.PS[0:NB, 0, 0:P]).then_inc(smp_step, 1)
                dve.tensor_copy(VS, m.PS[0:NB, 0, P:P + V]).then_inc(smp_step, 1)
                dve.wait_ge(smp_step, h * 4 + 2 + ONE)
                dve.tensor_tensor(KM, bc(KS8.unsqueeze(1), NB, P),
                                  bc(m.ident[0:NB, 0:NB].unsqueeze(2), NB, P), ALU.mult).then_inc(smp_step, 1)
                dve.tensor_tensor(QM, bc(qT[:, SEQ:TOK].unsqueeze(1), NB, NB), m.eye8[:], ALU.mult).then_inc(smp_step, 1)
                dve.wait_ge(pst_out, h * 16 + ONE)
                dve.memset(S[:, 0], 0.0).then_inc(s_ready, 1)

                def queries(c):
                    dve.wait_ge(ex_ready, h * QT + c + 1 + ONE)
                    dve.tensor_copy(DEC[:, c:c + 1], EX[:, 0, P - 1:P]).then_inc(qs_ready, 1)
                    if c >= 2:
                        dve.wait_ge(o_ready, h * QT + c - 1 + ONE)
                    dve.tensor_tensor(QS[:, c % 2], EX[:, 0:LEVELS + 1],
                                      bc(qT[:, c * P:(c + 1) * P].unsqueeze(1), LEVELS + 1, P),
                                      ALU.mult).then_inc(qs_ready, 1)

                def state(c):
                    dve.wait_ge(u_ready, h * QT + c + 1 + ONE)
                    dve.wait_ge(s_ready, h * (QT + 1) + c + 1 + ONE)
                    if c >= 1:
                        dve.wait_ge(o_ready, h * QT + c + ONE)
                    dve.scalar_tensor_tensor(out=S[:, (c + 1) % 2], in0=S[:, c % 2], scalar=DEC[:, c:c + 1],
                                             in1=m.PS[:, 2, 0:V], op0=ALU.mult, op1=ALU.add).then_inc(s_ready, 1)

                queries(0)
                for c in range(QT):
                    if c + 1 < QT:
                        queries(c + 1)
                    if c >= 1:
                        state(c - 1)
                    dve.wait_ge(a_ready, h * QT + c + 1 + ONE)
                    dve.tensor_tensor(AM, b_y.rearrange("p (a b) -> p a b", b=P), m.lmask[:], ALU.mult)\
                       .then_inc(am_ready, 1)
                    dve.wait_ge(am_ready, h * QT + c + 1 + ONE)
                    dve.tensor_reduce(AS[:, c % 2], AM.rearrange("p l t -> p t l"), AX_X, ALU.add)\
                       .then_inc(as_ready, 1)
                state(QT - 1)
                dve.wait_ge(fs_ready, h + 1 + ONE)
                for g in range(NG):
                    dve.wait_ge(st_in, (h * NG + g + 1) * 16 + ONE)
                    dve.wait_ge(outer_ready, h * NG + g + 1 + ONE)
                    for b in range(NBG):
                        n = g * NBG + b
                        dve.scalar_tensor_tensor(out=S0[:, b], in0=S0[:, b], scalar=FS[:, n:n + 1],
                                                 in1=b_x[:, b * V:(b + 1) * V], op0=ALU.mult, op1=ALU.add)\
                           .then_inc(st_ready, 1)
                dve.wait_ge(sq_ready, (h + 1) * (QT + 2) + ONE)
                dve.reciprocal(SSQ, SSQ).then_inc(on_step, 1)
                dve.wait_ge(on_step, h * 2 + 1 + ONE)
                dve.tensor_tensor(ON, ON, bc(SSQ.unsqueeze(2), QT + 1, V), ALU.mult).then_inc(on_step, 1)
                for v in range(VT):
                    for b in range(3):
                        dve.wait_ge(turn_ready, (h * VT + v) * 3 + b + 1 + ONE)
                        t0, t1 = (b * 512, b * 512 + 512) if b < 2 else (SEQ, TOK)
                        n = v * 3 + b
                        dve.scalar_tensor_tensor(out=m.O[:, ds(h * VT + v, 1), t0:t1],
                                                 in0=m.PS[:, 6 + n % 2:7 + n % 2, 0:t1 - t0], scalar=GN[:, v:v + 1],
                                                 in1=gT[:, v:v + 1, t0:t1], op0=ALU.mult, op1=ALU.mult)\
                           .then_inc(turn_read, 1)
    m.t += HEADS * NTL


def attention_memory(m):
    W = m.WR[:].rearrange("p a b -> p (a b)")
    m.VN = carve(W, 0, (2, QT, P))
    m.DIST = carve(W, 2048, (SEQ,))
    m.CAUSAL = carve(W, 3072, (SEQ,))
    m.WINDOW = carve(W, 4096, (WIN + P,))
    m.CDIST = carve(W, 4736, (QT, PBLK))
    m.CNEG = carve(W, 4864, (QT, PBLK))
    m.CVALID = carve(W, 4992, (QT, PBLK))
    m.NSL = carve(W, 5120, (R, G))
    r = NNSA * TOK
    m.W1D = carve(m.AR, r, (2, BLK, DH))
    m.W2D = carve(m.AR, r + 8192, (2, DH))
    m.PET = carve(m.AR, r + 8320, (2, BLK))
    m.HC = carve(m.AR, r + 8448, (2, G * PBLK), 0, DH)
    m.QP = carve(m.AR, r, (G, SEQ))
    m.AS = carve(m.AR, r + 2048, (G, SEQ))
    m.SS = carve(m.AR, r + 4096, (2, SEQ))
    m.PT = carve(m.AR, r + 6144, (2, QT, P))
    m.PC = carve(m.OT, 3328, (QT, G, 32))
    m.KCZ = carve(m.OT, 0, (2, G, SEQ))
    m.OH = carve(m.OT, 0, (QT, P))
    m.AW = carve(m.OT, 1024, (G, WIN + P))
    m.PCT = carve(m.OT, 2304, (QT, P), 0, DH)
    m.SC = carve(m.AR, r + 8192, (QT, G, PBLK))
    m.KCT = carve(m.keep, 0, (PBLK,))
    m.VCB = carve(m.keep, 16, (P,), 0, DH)
    m.GN = carve(m.keep, 144, (QT, 3, R, G))
    m.GR = carve(m.OT, 3840, (QT, 3, G))
    m.MC = carve(m.OT, 3888, (QT, G))
    m.RC = carve(m.OT, 3904, (QT, G))
    m.MX = carve(m.OT, 3920, (32,))
    m.GR2 = carve(m.OT, 3984, (QT, 2, G))
    m.SM = carve(m.OT, 3952, (32,))


def prepare_attention(nc, m, d):
    NT = m.NT
    with (nc.semaphore("z_ready") as z_ready,
          nc.semaphore("h_sum") as h_sum, nc.semaphore("h_ready") as h_ready,
          nc.semaphore("c_sum") as c_sum, nc.semaphore("c_read") as c_read,
          nc.semaphore("rows_out") as rows_out, nc.semaphore("v_turned") as v_turned, nc.semaphore("g_turned") as g_turned, nc.Block() as block):
        @block.sync
        def _(sp):
            sp.dma_start(d["kv_new"], NT[:, TKC:TGATE]).then_inc(rows_out, 16)
            sp.dma_start(d["win_kept"], d["win_rows"][:, 1:, :]).then_inc(rows_out, 16)
            sp.wait_ge(rows_out, 32)

        @block.gpsimd
        def _(pool):
            c = m.pool
            c.up(pool.iota(m.DIST, pattern=[[-1, SEQ]], base=SEQ - P, channel_multiplier=1,
                           allow_small_or_imprecise_dtypes=True))
            c.up(pool.iota(m.CDIST, pattern=[[P, QT], [-BLK, PBLK]], base=1 - BLK, channel_multiplier=1,
                           allow_small_or_imprecise_dtypes=True))
            c.up(pool.memset(m.CAUSAL, 0.0))
            c.up(pool.memset(m.WINDOW, 0.0))
            c.up(pool.memset(m.CNEG, 0.0))
            c.chain(pool, pool.memset(m.CVALID, 1.0))

            def select(view, base, pattern, mult, fill):
                c.chain(pool, pool.affine_select(out=view, in_=view, compare_op=ALU.is_ge, fill=fill, base=base,
                                                 pattern=pattern, channel_multiplier=mult))

            select(m.CAUSAL, SEQ - P, [[-1, SEQ]], 1, NEG)
            select(m.WINDOW, WIN, [[-1, WIN + P]], 1, NEG)
            select(m.WINDOW, -1, [[1, WIN + P]], -1, NEG)
            select(m.CNEG, 1 - BLK, [[P, QT], [-BLK, PBLK]], 1, NEG)
            select(m.CVALID, 1 - BLK, [[P, QT], [-BLK, PBLK]], 1, 0.0)

        @block.vector
        def _(dve):
            dve.wait_ge(m.w_cmp_in, 7 * 16)
            for kv in range(2):
                for g in range(G):
                    half = slice(g * DH, (g + 1) * DH)
                    dve.tensor_tensor(m.KCZ[half, kv, g].rearrange("p (b l) -> p b l", l=BLK),
                                      NT[half, TKC + kv, 0:SEQ].rearrange("p (b l) -> p b l", l=BLK),
                                      m.PET[half, kv].unsqueeze(1).to_broadcast([DH, PBLK, BLK]), ALU.add)\
                       .then_inc(z_ready, 1)
            dve.wait_ge(c_sum, 2)
            dve.tensor_copy(m.KCT, m.PS[:, 2, 0:PBLK]).then_inc(c_read, 1)
            for g in range(G):
                dve.tensor_copy(m.VCB[32 * g:32 * g + PBLK, g * DH:(g + 1) * DH],
                                m.PS[32 * g:32 * g + PBLK, 3, 0:DH]).then_inc(c_read, 1)
            dve.wait_ge(g_turned, 1)
            dve.tensor_copy(m.GN.rearrange("p a b c d -> p a (b c d)"),
                            m.PS[:, 1, 0:QT * 32].rearrange("p (a b) -> p a b", b=32)[:, :, 0:24]).then_inc(c_read, 1)

        @block.tensor
        def _(pe):
            pe.wait_ge(m.w_cmp_in, 7 * 16)
            for kv in range(2):
                pe.wait_ge(z_ready, 2 * kv + 2)
                z = m.KCZ[:, kv].rearrange("p g (b l) -> p l g b", l=BLK)
                for l in range(BLK):
                    mm = pe.matmul(m.PS[0:DH, kv, 0:G * PBLK], m.W1D[:, kv, l], z[:, l],
                                   start=(l == 0), stop=(l == BLK - 1))
                mm.then_inc(h_sum, 1)
            for kind in range(2):
                for j in range(QT):
                    mm = pe.transpose(m.PS[:, 4 + kind * 2 + j // 4, j % 4 * P:(j % 4 + 1) * P],
                                      NT[:, TVS if kind == 0 else TVW, j * P:(j + 1) * P], m.ident[:])
                    if j % 4 == 3:
                        mm.then_inc(v_turned, 1)
            pe.wait_ge(h_ready, 2)
            for j in range(QT):
                mm = pe.transpose(m.PS[:, 1, j * 32:j * 32 + 24], NT[0:24, TGATE, j * P:(j + 1) * P],
                                  m.ident[0:24, 0:24])
            mm.then_inc(g_turned, 1)
            for g in range(G):
                mm = pe.matmul(m.PS[g * DH:(g + 1) * DH, 2, 0:PBLK], m.W2D[0:DH, 0], m.HC[:, 0, g * PBLK:(g + 1) * PBLK],
                               start=True, stop=True)
            mm.then_inc(c_sum, 1)
            for g in range(G):
                mm = pe.matmul(m.PS[32 * g:32 * g + PBLK, 3, 0:DH], m.HC[:, 1, g * PBLK:(g + 1) * PBLK],
                               m.W2D[0:DH, 1], start=True, stop=True)
            mm.then_inc(c_sum, 1)

        @block.scalar
        def _(act):
            for kv in range(2):
                act.wait_ge(h_sum, kv + 1)
                act.activation(m.HC[:, kv], m.PS[0:DH, kv, 0:G * PBLK], ACT.Silu).then_inc(h_ready, 1)
            for n in range(4):
                act.wait_ge(v_turned, n + 1)
                m.act.up(act.activation(m.VN[:, n // 2, n % 2 * 4:n % 2 * 4 + 4],
                                        m.PS[:, 4 + n, :].rearrange("p (a b) -> p a b", b=P), ACT.Copy))


def attention(nc, m, d):
    assert PBLK <= TOPK
    NT, SS, PT, VN = m.NT, m.SS, m.PT, m.VN
    STEPS = [(g, kind, i) for g in range(G) for kind in range(2) for i in range(QT)]
    NS = len(STEPS)
    first_key = [0 if kind == 0 else max(0, i - WIN // P) for g, kind, i in STEPS]
    ntile = [i + 1 - f for (g, kind, i), f in zip(STEPS, first_key)]
    ngroup = [-(-n // 4) for n in ntile]
    before = np.cumsum([0] + ngroup).tolist()
    NGR = before[-1]
    assert NGR % 2 == 0

    def sbank(s):
        return m.PS[:, s % 2 * 2:s % 2 * 2 + 2].rearrange("p a b -> p (a b)")

    with phase(nc, "attention") as (ctx, sem, sems):
        q_ready = sem("q_ready")
        bias_ready = sem("bias_ready")
        cs_ready = sem("cs_ready")
        cp_step = sem("cp_step")
        cexp_ready = sem("cexp_ready")
        cpt_ready = sem("cpt_ready")
        cpt_read = sem("cpt_read")
        co_ready = sem("co_ready")
        co_read = sem("co_read")
        qk_ready = sem("qk_ready")
        s_ready = sem("s_ready")
        p_ready = sem("p_ready")
        pt_ready = sem("pt_ready")
        pt_read = sem("pt_read")
        pv_ready = sem("pv_ready")
        gr_ready = sem("gr_ready")
        coef_ready = sem("coef_ready")
        o_added = sem("o_added")
        ot_ready = sem("ot_ready")
        ot_read = sem("ot_read")
        zeroed = m.dve.n + 2
        block = ctx.enter_context(started(nc, sems))

        @block.tensor
        def _(pe):
            with pe.Fori(0, R) as r:
                def scores(s):
                    g, kind, i = STEPS[s]
                    k0, k1 = first_key[s] * P, (i + 1) * P
                    if s < 2:
                        pe.wait_ge(ot_read, r * 2 + ONE)
                    pe.wait_ge(s_ready, r * NS + max(s - 1, 0) + ONE)
                    for a in range(k0, k1, 512):
                        b = min(a + 512, k1)
                        mm = pe.matmul(sbank(s)[:, a - k0:b - k0], m.QP[:, g, i * P:(i + 1) * P],
                                       NT[:, TKS if kind == 0 else TKW, a:b], start=True, stop=True)
                    mm.then_inc(qk_ready, 1)

                def turn_probs(s):
                    pe.wait_ge(p_ready, r * NS + s + 1 + ONE)
                    for b in range(ngroup[s]):
                        n = before[s] + b
                        pe.wait_ge(pt_read, r * NGR + max(n - 1, 0) + ONE)
                        for j in range(b * 4, min(b * 4 + 4, ntile[s])):
                            mm = pe.transpose(m.PS[:, 4 + n % 2, (j % 4) * P:(j % 4 + 1) * P],
                                              SS[:, s % 2, j * P:(j + 1) * P], m.ident[:])
                        mm.then_inc(pt_ready, 1)

                def values(s):
                    g, kind, i = STEPS[s]
                    pe.wait_ge(pt_read, r * NGR + before[s] + ngroup[s] + ONE)
                    pe.wait_ge(o_added, r * NS + max(s - 1, 0) + ONE)
                    for j in range(ntile[s]):
                        mm = pe.matmul(m.PS[:, 6 + s % 2, 0:P], PT[:, s % 2, j], VN[:, kind, first_key[s] + j],
                                       start=(j == 0), stop=(j == ntile[s] - 1))
                    mm.then_inc(pv_ready, 1)

                pe.wait_ge(q_ready, (r + 1) * 2 + ONE)
                pe.wait_ge(o_added, r * NS + ONE)
                for i in range(QT):
                    for g in range(G):
                        c0 = (i * G + g) * PBLK
                        mm = pe.matmul(m.PS[:, 7, c0:c0 + PBLK], m.QP[:, g, i * P:(i + 1) * P], m.KCT,
                                       start=True, stop=True)
                mm.then_inc(cs_ready, 1)
                pe.wait_ge(cp_step, (r + 1) * 9 + ONE)
                scores(0)
                for b in range(2):
                    for i in range(b * 4, b * 4 + 4):
                        mm = pe.transpose(m.PS[0:DH, 4 + b, i % 4 * P:(i % 4 + 1) * P],
                                          m.PC[:, i].rearrange("p a b -> p (a b)"), m.ident[:])
                    mm.then_inc(cpt_ready, 1)
                for b in range(2):
                    pe.wait_ge(cpt_read, r * 2 + b + 1 + ONE)
                    for i in range(b * 4, b * 4 + 4):
                        mm = pe.matmul(m.PS[:, 6 + b, i % 4 * P:(i % 4 + 1) * P], m.PCT[:, i], m.VCB, start=True, stop=True)
                    mm.then_inc(co_ready, 1)
                pe.wait_ge(co_read, r * 2 + 2 + ONE)
                for s in range(NS):
                    if s + 1 < NS:
                        scores(s + 1)
                    turn_probs(s)
                    if s >= 1:
                        values(s - 1)
                values(NS - 1)
                pe.wait_ge(o_added, (r + 1) * NS + ONE)
                for b in range(2):
                    for i in range(b * 4, b * 4 + 4):
                        mm = pe.transpose(m.PS[:, b, i % 4 * P:(i % 4 + 1) * P], m.OH[:, i], m.ident[:])
                    mm.then_inc(ot_ready, 1)

        @block.scalar
        def _(act):
            with act.Fori(0, R) as r:
                act.wait_ge(m.dve.sem, zeroed)
                act.wait_ge(qk_ready, r * NS + ONE)
                for g in range(G):
                    half = slice(g * DH, (g + 1) * DH)
                    act.activation(m.QP[half, g:g + 1], NT[half, ds(r, 1), 0:SEQ], ACT.Copy).then_inc(q_ready, 1)
                act.wait_ge(cp_step, r * 9 + 3 + ONE)
                act.activation(m.SC, m.SC, ACT.Exp).then_inc(cexp_ready, 1)
                for b in range(2):
                    act.wait_ge(cpt_ready, r * 2 + b + 1 + ONE)
                    act.activation(m.PCT[:, b * 4:b * 4 + 4], m.PS[0:DH, 4 + b, :].rearrange("p (a b) -> p a b", b=P),
                                   ACT.Copy).then_inc(cpt_read, 1)

                def expo(s):
                    n = ntile[s] * P
                    act.wait_ge(s_ready, r * NS + s + 1 + ONE)
                    act.activation(SS[:, s % 2, 0:n], SS[:, s % 2, 0:n], ACT.Exp, bias=m.MX[:, s:s + 1], scale=-1.0,
                                   accum_out=m.SM[:, s:s + 1]).then_inc(p_ready, 1)

                expo(0)
                for s in range(NS):
                    if s + 1 < NS:
                        expo(s + 1)
                    for b in range(ngroup[s]):
                        n = before[s] + b
                        act.wait_ge(pt_ready, r * NGR + n + 1 + ONE)
                        act.wait_ge(pv_ready, r * NS + max(s - 1, 0) + ONE)
                        j0, j1 = b * 4, min(b * 4 + 4, ntile[s])
                        act.activation(PT[:, s % 2, j0:j1],
                                       m.PS[:, 4 + n % 2, 0:(j1 - j0) * P].rearrange("p (a b) -> p a b", b=P),
                                       ACT.Copy).then_inc(pt_read, 1)
                for b in range(2):
                    act.wait_ge(ot_ready, r * 2 + b + 1 + ONE)
                    act.activation(m.O[:, ds(r + HEADS, 1), b * 512:b * 512 + 512], m.PS[:, b:b + 1, :], ACT.Copy)\
                       .then_inc(ot_read, 1)

        @block.vector
        def _(dve):
            t = m.dve
            t.up(dve.memset(m.QP, 0.0))
            t.up(dve.memset(m.PC, 0.0))
            dve.wait_ge(t.sem, zeroed)

            def pbc(x):
                return x.unsqueeze(3).to_broadcast([P, QT, G, PBLK])

            def cbc(x):
                return x.unsqueeze(2).to_broadcast([P, QT, G, PBLK])

            with dve.Fori(0, R) as r:
                def score_waits(s):
                    dve.wait_ge(qk_ready, r * NS + s + 1 + ONE)
                    dve.wait_ge(pt_ready, r * NGR + (before[s - 1] if s else 0) + ONE)

                def score(s):
                    g, kind, i = STEPS[s]
                    n = ntile[s] * P
                    bias = m.AS[:, g, SEQ - n:SEQ] if kind == 0 else m.AW[:, g, WIN + P - n:WIN + P]
                    dve.tensor_tensor_reduce(SS[:, s % 2, 0:n], sbank(s)[:, 0:n], bias, -1.0, 3e38, ALU.add, ALU.min,
                                             m.MX[:, s:s + 1]).then_inc(s_ready, 1)

                for g in range(G):
                    slope = m.NSL[:, ds(r, 1), g:g + 1].rearrange("p a b -> p (a b)")
                    dve.wait_ge(s_ready, r * NS + ONE)
                    dve.scalar_tensor_tensor(out=m.AS[:, g], in0=m.DIST, scalar=slope, in1=m.CAUSAL,
                                             op0=ALU.mult, op1=ALU.add).then_inc(bias_ready, 1)
                    dve.scalar_tensor_tensor(out=m.AW[:, g], in0=m.DIST[:, SEQ - WIN - P:SEQ], scalar=slope,
                                             in1=m.WINDOW, op0=ALU.mult, op1=ALU.add).then_inc(bias_ready, 1)
                    dve.wait_ge(cpt_ready, r * 2 + ONE)
                    dve.scalar_tensor_tensor(out=m.SC[:, :, g], in0=m.CDIST, scalar=slope, in1=m.CNEG,
                                             op0=ALU.mult, op1=ALU.add).then_inc(bias_ready, 1)
                dve.wait_ge(coef_ready, r * NS * 2 + ONE)
                dve.tensor_copy(m.GR, m.GN.rearrange("p a b r g -> p (a b) r g")[:, :, ds(r, 1), :]
                                .rearrange("p a r g -> p a (r g)").rearrange("p (a b) g -> p a b g", b=3))\
                   .then_inc(bias_ready, 1)
                dve.wait_ge(bias_ready, (r + 1) * 7 + ONE)
                dve.wait_ge(cs_ready, r + 1 + ONE)
                dve.tensor_tensor(m.SC, m.SC, m.PS[:, 7, 0:256].rearrange("p (a b c) -> p a b c", a=QT, b=G), ALU.add)\
                   .then_inc(cp_step, 1)
                dve.wait_ge(cp_step, r * 9 + 1 + ONE)
                dve.tensor_reduce(m.MC, m.SC, AX_X, ALU.max).then_inc(cp_step, 1)
                dve.wait_ge(cp_step, r * 9 + 2 + ONE)
                dve.tensor_tensor(m.SC, m.SC, pbc(m.MC), ALU.subtract).then_inc(cp_step, 1)
                dve.wait_ge(cexp_ready, r + 1 + ONE)
                dve.tensor_tensor(m.SC, m.SC, cbc(m.CVALID), ALU.mult).then_inc(cp_step, 1)
                dve.wait_ge(cp_step, r * 9 + 4 + ONE)
                dve.tensor_reduce(m.RC, m.SC, AX_X, ALU.add).then_inc(cp_step, 1)
                dve.wait_ge(cp_step, r * 9 + 5 + ONE)
                dve.tensor_scalar(m.RC, m.RC, TINY, None, ALU.max).then_inc(cp_step, 1)
                dve.wait_ge(cp_step, r * 9 + 6 + ONE)
                dve.reciprocal(m.RC, m.RC).then_inc(cp_step, 1)
                dve.wait_ge(cp_step, r * 9 + 7 + ONE)
                dve.tensor_tensor(m.RC, m.RC, m.GR[:, :, 0], ALU.mult).then_inc(cp_step, 1)
                dve.wait_ge(cp_step, r * 9 + 8 + ONE)
                dve.tensor_tensor(m.PC[:, :, :, 0:PBLK], m.SC, pbc(m.RC), ALU.mult).then_inc(cp_step, 1)
                for b in range(2):
                    dve.wait_ge(co_ready, r * 2 + b + 1 + ONE)
                    dve.wait_ge(ot_ready, r * 2 + ONE)
                    if b == 1:
                        score_waits(0)
                    dve.tensor_copy(m.OH[:, b * 4:b * 4 + 4], m.PS[:, 6 + b, :].rearrange("p (a b) -> p a b", b=P))\
                       .then_inc(co_read, 1)

                def add(s):
                    g, kind, i = STEPS[s]
                    part = m.OH[:, i, g * DH:(g + 1) * DH]
                    dve.wait_ge(coef_ready, (r * NS + s + 1) * 2 + ONE)
                    dve.wait_ge(pv_ready, r * NS + s + 1 + ONE)
                    if kind == 0:
                        dve.wait_ge(co_read, r * 2 + 2 + ONE)
                    else:
                        dve.wait_ge(o_added, r * NS + s - QT + 1 + ONE)
                    dve.scalar_tensor_tensor(out=part, in0=m.PS[:, 6 + s % 2, g * DH:(g + 1) * DH],
                                             scalar=m.SM[:, s:s + 1], in1=part, op0=ALU.mult, op1=ALU.add)\
                       .then_inc(o_added, 1)

                def invert(s):
                    dve.wait_ge(p_ready, r * NS + s + 1 + ONE)
                    if s + 2 < NS:
                        score_waits(s + 2)
                    dve.reciprocal(m.SM[:, s:s + 1], m.SM[:, s:s + 1]).then_inc(coef_ready, 1)

                score(0)
                score_waits(1)
                dve.tensor_copy(m.GR2, m.GR[:, :, 1:3]).then_inc(gr_ready, 1)
                score(1)
                for s in range(NS):
                    g, kind, i = STEPS[s]
                    invert(s)
                    if s + 2 < NS:
                        score(s + 2)
                    dve.wait_ge(gr_ready, r + 1 + ONE)
                    dve.wait_ge(coef_ready, (r * NS + s) * 2 + 1 + ONE)
                    dve.tensor_tensor(m.SM[:, s:s + 1], m.SM[:, s:s + 1], m.GR2[:, i, kind, g:g + 1], ALU.mult)\
                       .then_inc(coef_ready, 1)
                    if s >= 1:
                        add(s - 1)
                add(NS - 1)


C_SEL, C_SHIFT, C_RM, C_NSL, C_GM, C_GJ, C_PAR, C_J, C_TRI, C_S, C_L, C_CD, C_END = np.cumsum(
    [0, 256, 256, 16, 1, 64, 3, 1, 1, 128, 16, 64, 128]).tolist()
NBG16 = NB * G


def sample_memory(m):
    W = m.WR[:].rearrange("p a b -> p (a b)")
    at = [0]

    def o(*shape, parts=P, t=m.OT):
        v = carve(t, at[0], shape, 0, parts)
        at[0] += int(np.prod(shape))
        return v

    m.SN = o(NNSA, NB)
    m.QM = o(17 * ROWS)
    m.QD = o(G, R, NB)
    m.SD = o(G, 4, NB)
    m.QR = o(ROWS, parts=DH)
    m.GX = o(NB, G * R, parts=24)
    m.GS = o(3, parts=ROWS)
    m.CT = o(C_END)
    m.OWT = o(ROWS, parts=DH)
    m.HS = o(2, 2, G, BLK, parts=DH)
    m.RT = o(16, parts=ROWS)
    m.S16 = o(2, NBG16, parts=ROWS)
    m.DG = o(ROWS, parts=ROWS)
    assert at[0] <= 4 * TOK, at[0]
    m.KW = carve(m.AR, 0, (NBG16, WIN // 2))
    m.VW = carve(m.AR, 4096, (NBG16, WIN // P, DH))
    m.SW = carve(m.AR, 8192, (WIN + 1,), 0, ROWS)
    m.BW = carve(m.AR, 8192 + 520, (WIN,), 0, ROWS)
    m.WD = carve(m.AR, 8192 + 1552, (WIN,), 0, ROWS)
    m.PWT = carve(m.AR, 8192 + 1040, (WIN // P, ROWS))
    m.PB = carve(m.AR, 0, (2, NPG // 2, 2, 32, 4))
    m.KCS = carve(m.AR, 16384, (NBG16, SBLK), 0, DH)
    m.VCS = carve(m.AR, 18432, (NBG16, DH))
    m.W1C = carve(W, 0, (2, 32, DH))
    m.PEJ = carve(W, 4096, (2, 32))
    m.W2C = carve(W, 4160, (2, DH), 0, DH)
    m.BIA = carve(W, 4288, (2,), 0, DH)
    m.PTAB = carve(W, 4296, (NB * NPG,), 0, 1).bitcast(I32)
    m.KVG = carve(m.AR, 0, (NB, G, TOPK // 2, P))
    m.PCR = carve(W, 0, (SBLK,), 0, ROWS)
    m.IMP = carve(W, 128, (NBG16,))
    m.RK = carve(W, 144, (NBG16,))
    m.EQ = carve(W, 160, (2, SBLK))
    m.OHS = carve(W, 416, (NB, G, TOPK))
    m.WBJ = carve(W, 672, (2, NB, G, TOPK))
    m.PTJ = carve(W, 1184, (NB,)).bitcast(I32)
    m.BAS = carve(W, 1192, (NB,))
    m.IDX = carve(W, 1200, (NBG16 * TOPK,), 0, 1).bitcast(I32)
    m.BRX = carve(W, 1456, (NBG16, TOPK), 0, ROWS)
    m.BR = carve(W, 1712, (TOPK,), 0, ROWS)
    m.BI = carve(W, 1728, (2, 8, BLK), 0, ROWS)
    m.SL = carve(W, 2752, (TOPK * BLK + 1,), 0, ROWS)
    m.PLT = carve(W, 3780, (8, ROWS))
    m.PCTT = carve(W, 4292, (ROWS,))
    m.OT = carve(W, 4356, (ROWS,), 0, DH)
    m.TV = carve(W, 4420, (ROWS,), 0, DH)


def sample_window(nc, m, d):
    C = m.CT
    with phase(nc, "window") as (ctx, sem, sems):
        table_in, win_in = sem("table_in"), sem("win_in")
        sn_ready = sem("sn_ready")
        pe_step, act_step = sem("pe_step"), sem("act_w")
        gx_ready = sem("gx_ready")
        qm_ready = sem("qm_ready")
        sw_ready = sem("sw_ready")
        pw_ready = sem("pw_ready")
        pt_ready = sem("pt_ready")
        block = ctx.enter_context(nc.Block())

        @block.sync
        def _(sp):
            sp.dma_start(C, d["table"]).then_inc(table_in, 16)
            sp.dma_start(m.WD, d["win_dist"]).then_inc(table_in, 16)
            sp.wait_ge(sn_ready, 1)
            sp.dma_start(m.KW, d["win_k"]).then_inc(win_in, 16)
            sp.dma_start(m.VW, d["win_v"]).then_inc(win_in, 16)

        @block.scalar
        def _(act):
            act.activation(m.SN, m.NT[:, :, SEQ:TOK], ACT.Copy).then_inc(sn_ready, 1)
            act.wait_ge(sw_ready, 1)
            act.activation(m.SW, m.SW, ACT.Exp, bias=m.RT[:, 0:1], scale=-1.0, accum_out=m.RT[:, 1:2])\
               .then_inc(act_step, 1)
            act.wait_ge(pe_step, 4)
            act.activation(m.PWT, m.PS[:, 4, 0:WIN // P * ROWS].rearrange("p (a b) -> p a b", b=ROWS), ACT.Copy)\
               .then_inc(act_step, 1)

        @block.tensor
        def _(pe):
            pe.wait_ge(table_in, 32)
            pe.wait_ge(sn_ready, 1)
            for g in range(G):
                sel = C[:, C_SEL + g * P:C_SEL + (g + 1) * P]
                pe.matmul(m.PS[:, 0, g * 64:g * 64 + 32], sel, m.SN[:, TQ:TQ + R].rearrange("p a b -> p (a b)"),
                          start=True, stop=True)
                mm = pe.matmul(m.PS[:, 0, g * 64 + 32:g * 64 + 64], sel,
                               m.SN[:, TKS:TKS + 4].rearrange("p a b -> p (a b)"), start=True, stop=True)
            mm.then_inc(pe_step, 1)
            pe.wait_ge(gx_ready, 1)
            pe.matmul(m.PS[0:ROWS, 1, 0:3], m.GX.rearrange("p a b -> p (a b)"), C[0:24, C_GJ:C_GJ + 3],
                      start=True, stop=True).then_inc(pe_step, 1)
            pe.wait_ge(win_in, 32)
            pe.wait_ge(qm_ready, 3)
            for half in range(2):
                rows = slice(half * DH, (half + 1) * DH)
                for n in range(NBG16):
                    pe.matmul(m.PS[0:ROWS, 2 if half == 0 else 7, 0:WIN // 2], m.QM[rows, n * ROWS:(n + 1) * ROWS],
                              m.KW[rows, n], start=(n == 0), stop=(n == NBG16 - 1))
            for kind in range(2):
                mm = pe.matmul(m.PS[0:ROWS, 3, kind * NBG16:(kind + 1) * NBG16], m.QR,
                               m.SD[0:DH, :, 2 * kind].rearrange("p g b -> p b g"), start=True, stop=True)
            mm.then_inc(pe_step, 1)
            pe.wait_ge(pw_ready, 1)
            for c in range(WIN // P):
                mm = pe.transpose(m.PS[:, 4, c * ROWS:(c + 1) * ROWS], m.SW[:, c * P:(c + 1) * P], m.ident[0:ROWS, 0:ROWS])
            mm.then_inc(pe_step, 1)
            pe.wait_ge(act_step, 2)
            for n in range(NBG16):
                for c in range(WIN // P):
                    mm = pe.matmul(m.PS[0:DH, 5, n * R:(n + 1) * R], m.VW[:, n, c], m.PWT[:, c, n * R:(n + 1) * R],
                                   start=(c == 0), stop=(c == WIN // P - 1))
            pe.wait_ge(pw_ready, 2)
            pe.matmul(m.PS[0:DH, 6, 0:ROWS], m.ones[0:ROWS, 0:DH], m.DG, start=True, stop=True).then_inc(pe_step, 1)

        @block.vector
        def _(dve):
            t = m.dve
            t.up(dve.memset(m.QM, 0.0))
            dve.wait_ge(sn_ready, 1)
            dve.wait_ge(table_in, 32)
            dve.tensor_tensor(m.GX, m.SN[0:24, TGATE].unsqueeze(2).to_broadcast([24, NB, G * R]),
                              C[0:24, C_GM:C_GM + ROWS].rearrange("p (a b) -> p a b", b=G * R), ALU.mult)\
               .then_inc(gx_ready, 1)
            dve.wait_ge(pe_step, 1)
            ps = m.PS[:, 0, 0:128].rearrange("p (g k n) -> p g k n", g=G, k=2)
            dve.tensor_copy(m.QD.rearrange("p g r b -> p g (r b)"), ps[:, :, 0]).then_inc(qm_ready, 1)
            dve.tensor_copy(m.SD.rearrange("p g k b -> p g (k b)"), ps[:, :, 1]).then_inc(qm_ready, 1)
            dve.wait_ge(qm_ready, 2)
            dve.wait_ge(t.sem, t.n)
            diag = m.QM[:, 0:NBG16 * (ROWS + R)].rearrange("p (b g c) -> p b g c", b=NB, g=G)[:, :, :, 0:R]
            t.up(dve.tensor_copy(diag, m.QD.rearrange("p g r b -> p b g r")))
            dve.wait_ge(t.sem, t.n)
            dve.tensor_copy(m.QR.rearrange("p (b g r) -> p b g r", b=NB, g=G),
                            m.QD[0:DH].rearrange("p g r b -> p b g r")).then_inc(qm_ready, 1)
            dve.wait_ge(pe_step, 2)
            t.up(dve.tensor_copy(m.GS, m.PS[0:ROWS, 1, 0:3]))
            t.chain(dve, dve.tensor_scalar(m.BW, m.WD, C[0:ROWS, C_NSL:C_NSL + 1], None, ALU.mult))
            t.chain(dve, dve.memset(m.BW[:, 0:1], NEG))
            dve.wait_ge(pe_step, 3)
            t.chain(dve, dve.tensor_tensor(m.S16, m.PS[0:ROWS, 3, 0:2 * NBG16].rearrange("p (a b) -> p a b", a=2),
                                           C[0:ROWS, C_RM:C_RM + NBG16].unsqueeze(1).to_broadcast([ROWS, 2, NBG16]),
                                           ALU.mult))
            t.chain(dve, dve.tensor_reduce(m.RT[:, 4:6], m.S16, AX_X, ALU.add))
            t.up(dve.tensor_scalar(m.SW[:, WIN:WIN + 1], m.RT[:, 5:6], -1.0, None, ALU.mult))
            for half, bank in ((0, 2), (1, 7)):
                cols = slice(half * WIN // 2, (half + 1) * WIN // 2)
                t.chain(dve, dve.tensor_tensor_reduce(m.SW[:, cols], m.PS[0:ROWS, bank, 0:WIN // 2], m.BW[:, cols], -1.0,
                                                      3e38, ALU.add, ALU.min, m.RT[:, 2 + half:3 + half]))
            t.chain(dve, dve.tensor_tensor(m.RT[:, 2:3], m.RT[:, 2:3], m.RT[:, 3:4], ALU.min))
            dve.tensor_tensor(m.RT[:, 0:1], m.RT[:, 2:3], m.SW[:, WIN:WIN + 1], ALU.min).then_inc(sw_ready, 1)
            dve.wait_ge(act_step, 1)
            t.chain(dve, dve.reciprocal(m.RT[:, 1:2], m.RT[:, 1:2]))
            t.chain(dve, dve.tensor_tensor(m.RT[:, 1:2], m.RT[:, 1:2], m.GS[:, 2:3], ALU.mult))
            dve.tensor_scalar(m.SW, m.SW, m.RT[:, 1:2], None, ALU.mult).then_inc(pw_ready, 1)
            dve.wait_ge(pw_ready, 1)
            dve.tensor_scalar(m.DG, m.ident[0:ROWS, 0:ROWS], m.SW[:, WIN:WIN + 1], None, ALU.mult).then_inc(pw_ready, 1)
            dve.wait_ge(pe_step, 5)
            v_new = m.SD[0:DH, :, 3].rearrange("p g b -> p b g").unsqueeze(3).to_broadcast([DH, NB, G, R])
            t.chain(dve, dve.tensor_tensor(m.OWT.rearrange("p (b g r) -> p b g r", b=NB, g=G),
                                           m.PS[0:DH, 6, 0:ROWS].rearrange("p (b g r) -> p b g r", b=NB, g=G),
                                           v_new, ALU.mult))
            t.chain(dve, dve.tensor_tensor(m.OWT, m.OWT, m.PS[0:DH, 5, 0:ROWS], ALU.add))


def sample_compress(nc, m, d):
    HALF = NPG // 2
    HEAD = ONE + 2
    with phase(nc, "compress") as (ctx, sem, sems):
        tab_in, w_in = sem("tab_in"), sem("w_cmp_in")
        page_in = [sem(f"page_in{u}") for u in range(2)]
        pool_in = [nc.alloc_semaphore(f"compress_pool_in{u}") for u in range(2)]
        pool_go = sem("pool_go")
        bias_sum, bias_ready = sem("bias_sum"), sem("bias_ready")
        h_sum = sem("h_sum")
        h_ready = sem("h_ready")
        c_sum = sem("c_sum")
        c_read = sem("c_read")
        block = ctx.enter_context(started(nc, sems + 2 * [h_sum, h_ready, c_sum]))

        def fetch(eng, b, u, first, count):
            for n in range(first, first + count, 4):
                pages = [eng.value_load(m.PTAB[0:1, ds(b * NPG + (n + k + u * HALF), 1)]) for k in range(4)]
                for k in range(4):
                    if n == first and k == 0 and eng is not nc.gpsimd:
                        eng.wait_ge(h_sum, b * 2 + u - 1 + HEAD)
                    eng.dma_start(m.PB[:, u, n + k:n + k + 1].rearrange("p n a b c -> p n (a b c)"),
                                  d["cmp"][ds(pages[k], 1)].rearrange("n p c -> p n c"))\
                        .then_inc((pool_in if eng is nc.gpsimd else page_in)[u], 16)

        @block.sync
        def _(sp):
            sp.dma_start(m.PTAB, d["pages"]).then_inc(tab_in, 16)
            sp.dma_start(m.W1C, d["w1_c"]).then_inc(w_in, 16)
            sp.dma_start(m.PEJ, d["pe_c"]).then_inc(w_in, 16)
            sp.dma_start(m.W2C, d["w2_hd"]).then_inc(w_in, 16)
            sp.wait_ge(tab_in, 16 + ONE)
            with sp.Fori(0, NB) as b:
                for u in range(2):
                    fetch(sp, b, u, 0, 12)

        @block.gpsimd
        def _(pool):
            pool.wait_ge(tab_in, 16 + ONE)
            with pool.Fori(0, NB) as b:
                for u in range(2):
                    pool.wait_ge(h_sum, b * 2 + u - 1 + HEAD)
                    pool.sem_inc(pool_go, 1)
                    fetch(pool, b, u, 12, 12)

        @block.tensor
        def _(pe):
            pe.wait_ge(w_in, 48 + ONE)
            for kv in range(2):
                for j in range(32):
                    mm = pe.matmul(m.PS[0:DH, 7, kv:kv + 1], m.W1C[:, kv, j], m.PEJ[:, kv, j:j + 1],
                                   start=(j == 0), stop=(j == 31))
            mm.then_inc(bias_sum, 1)
            with pe.Fori(0, NB) as b:
                for u in range(2):
                    pe.wait_ge(page_in[u], b * (20 * 16) + 20 * 16 + ONE)
                    pe.wait_ge(pool_in[u], b * (12 * 16) + 12 * 16)
                    pe.wait_ge(h_ready, b * 4 + (u - 1) * 2 + HEAD)
                    for kv in range(2):
                        for j in range(32):
                            mm = pe.matmul(m.PS[0:DH, u * 2 + kv, 0:P].rearrange("p (a b) -> p a b", b=4),
                                           m.W1C[:, kv, j], m.PB[:, u, :, kv, j], start=(j == 0), stop=(j == 31))
                    mm.then_inc(h_sum, 1)
                for u in range(2):
                    pe.wait_ge(h_ready, b * 4 + u * 2 + 2 + HEAD)
                    pe.wait_ge(c_read, b * 4 + u * 2 + ONE)
                    pe.matmul(m.PS[:, 4, 0:P], m.W2C.rearrange("p a b -> p (a b)"), m.HS[:, u, 0].rearrange("p a b -> p (a b)"),
                              start=True, stop=True)
                    for g in range(G):
                        mm = pe.matmul(m.PS[u * DH:(u + 1) * DH, 5, g * DH:(g + 1) * DH], m.HS[:, u, 1, g],
                                       m.W2C[:, 1], start=True, stop=True)
                    mm.then_inc(c_sum, 1)

        @block.scalar
        def _(act):
            def silu(b, u):
                act.wait_ge(h_sum, b * 2 + u + 1 + HEAD)
                act.wait_ge(c_sum, b * 2 + u - 1 + HEAD)
                for kv in range(2):
                    act.activation(m.HS[:, u, kv].rearrange("p g (n h) -> p n g h", h=2),
                                   m.PS[0:DH, u * 2 + kv, 0:P].rearrange("p (n g h) -> p n g h", g=G, h=2),
                                   ACT.Silu, bias=m.BIA[:, kv:kv + 1]).then_inc(h_ready, 1)

            act.wait_ge(tab_in, 16 + ONE)
            for u in range(2):
                fetch(act, 0, u, 24, 8)
            act.wait_ge(bias_ready, 1 + ONE)
            with act.Fori(0, NB - 1) as b:
                for u in range(2):
                    silu(b, u)
                    fetch(act, b + 1, u, 24, 8)
            for u in range(2):
                silu(NB - 1, u)

        @block.vector
        def _(dve):
            dve.wait_ge(bias_sum, 1 + ONE)
            dve.tensor_copy(m.BIA, m.PS[0:DH, 7, 0:2]).then_inc(bias_ready, 1)
            with dve.Fori(0, NB) as b:
                for u in range(2):
                    dve.wait_ge(c_sum, b * 2 + u + 1 + HEAD)
                    dve.tensor_copy(m.KCS[:, ds(b * G, G), u * BLK:(u + 1) * BLK],
                                    m.PS[0:DH, 4, 0:P].rearrange("p (a b) -> p a b", b=BLK)).then_inc(c_read, 1)
                    dve.tensor_copy(m.VCS[u * DH:(u + 1) * DH, ds(b * G, G)],
                                    m.PS[u * DH:(u + 1) * DH, 5, 0:P].rearrange("p (a b) -> p a b", b=DH))\
                       .then_inc(c_read, 1)


    nc.clear_and_free_semaphores(pool_in)
    nc.all_engine_barrier()


def sample_select(nc, m, d):
    C = m.CT
    NK = TOPK * BLK
    FETCHED = [g * TOPK + s for g in range(G) for s in range(TOPK - 1)]
    with phase(nc, "select") as (ctx, sem, sems):
        ptj_in = sem("ptj_in")
        cs_ready, cs_neg, ce_ready = sem("cs_ready"), sem("cs_neg"), sem("ce_ready")
        pc_ready = sem("pc_ready")
        imp_sum, imp_ready = sem("imp_sum"), sem("imp_ready")
        imp_rows = sem("imp_rows")
        rank_step = sem("rank_step")
        wb_ready = sem("wb_ready")
        ids_ready = sem("ids_ready")
        idx_ready = sem("idx_ready")
        blocks_in = sem("blocks_in")
        pool_in = sem("pool_in")
        ss_ready, ss_neg, se_ready = sem("ss_ready"), sem("ss_neg"), sem("se_ready")
        ps_ready = sem("ps_ready")
        pt_ready, pt_read = sem("pt_ready"), sem("pt_read")
        pg_ready = sem("pg_ready")
        o_ready, ot_ready, place_ready = sem("o_ready"), sem("ot_ready"), sem("place_ready")
        block = ctx.enter_context(nc.Block())

        def fetch(eng, slots):
            eng.wait_ge(idx_ready, 1)
            with eng.Fori(0, NB) as b:
                for n in range(0, len(slots), 4):
                    some = slots[n:n + 4]
                    rows = [eng.value_load(m.IDX[0:1, ds(b * (G * TOPK) + slot, 1)]) for slot in some]
                    for slot, row in zip(some, rows):
                        g, s = divmod(slot, TOPK)
                        half = slice(s % 2 * DH, s % 2 * DH + DH)
                        eng.dma_start(m.KVG[half, ds(b, 1), g, s // 2], d["slc"][ds(row, 1), g]
                                      .rearrange("n p c -> p n c"))\
                            .then_inc(pool_in if eng is nc.gpsimd else blocks_in, 16)

        @block.sync
        def _(sp):
            sp.dma_start(m.PTJ, d["block_page"]).then_inc(ptj_in, 16)
            fetch(sp, FETCHED[0:10])

        @block.gpsimd
        def _(pool):
            fetch(pool, FETCHED[20:30])

        @block.tensor
        def _(pe):
            for n in range(NBG16):
                mm = pe.matmul(m.PS[0:ROWS, 0, 0:SBLK], m.QM[0:DH, n * ROWS:(n + 1) * ROWS], m.KCS[:, n],
                               start=(n == 0), stop=(n == NBG16 - 1))
            mm.then_inc(cs_ready, 1)
            pe.wait_ge(pc_ready, 1)
            pe.matmul(m.PS[:, 1, 0:NBG16], m.PCR, C[0:ROWS, C_RM:C_RM + NBG16], start=True, stop=True)\
              .then_inc(imp_sum, 1)
            pe.wait_ge(imp_ready, 2)
            for n in range(NBG16):
                mm = pe.transpose(m.PS[:, 4 + n // 4, n % 4 * P:(n % 4 + 1) * P],
                                  m.IMP[:, n:n + 1].to_broadcast([P, P]), m.ident[:])
            mm.then_inc(imp_rows, 1)
            pe.wait_ge(wb_ready, 2)
            for k in range(2):
                mm = pe.matmul(m.PS[:, 2 + k, 0:256], m.ones[:], m.WBJ[:, k].rearrange("p a b c -> p (a b c)"),
                               start=True, stop=True)
            mm.then_inc(ids_ready, 1)
            pe.wait_ge(blocks_in, 20 * NB * 16)
            pe.wait_ge(pool_in, 10 * NB * 16)
            pe.wait_ge(idx_ready, 2)
            for half in range(2):
                rows = slice(half * DH, (half + 1) * DH)
                for n in range(NBG16):
                    mm = pe.matmul(m.PS[0:ROWS, 2 + half, :].rearrange("p (a b) -> p a b", b=BLK),
                                   m.QM[rows, n * ROWS:(n + 1) * ROWS], m.KVG[rows, n // G, n % G, :, 0:BLK],
                                   start=(n == 0), stop=(n == NBG16 - 1))
            mm.then_inc(ss_ready, 1)
            pe.wait_ge(pg_ready, 1)
            pe.transpose(m.PS[:, 1, 0:ROWS], m.PCR, m.ident[0:ROWS, 0:ROWS]).then_inc(pt_ready, 1)
            pe.wait_ge(ps_ready, 1)
            for c in range(TOPK // 2):
                mm = pe.transpose(m.PS[:, 4, c * ROWS:(c + 1) * ROWS],
                                  m.BI.rearrange("p a b c -> p (a b c)")[:, c * P:(c + 1) * P],
                                  m.ident[0:ROWS, 0:ROWS])
            mm.then_inc(pt_ready, 1)
            pe.wait_ge(pt_read, 2)
            for n in range(NBG16):
                rows = slice(n * R, (n + 1) * R)
                pe.matmul(m.PS[0:DH, 5, rows], m.VCS[:, n], m.PCTT[:, rows], start=True, stop=False)
                for c in range(TOPK // 2):
                    pe.matmul(m.PS[0:DH, 5, rows], m.KVG[:, n // G, n % G, c, BLK:], m.PLT[:, c, rows],
                              start=False, stop=(c == TOPK // 2 - 1))
            pe.wait_ge(ps_ready, 2)
            pe.matmul(m.PS[0:DH, 6, 0:ROWS], m.ones[0:ROWS, 0:DH], m.DG, start=True, stop=True).then_inc(o_ready, 1)
            pe.wait_ge(ot_ready, 1)
            for g in range(G):
                mm = pe.matmul(m.PS[:, 7, 0:R * NB], C[0:DH, C_SHIFT + g * P:C_SHIFT + (g + 1) * P],
                               m.OT.rearrange("p (b g r) -> p g r b", b=NB, g=G)[:, g], start=(g == 0), stop=(g == 1))
            mm.then_inc(place_ready, 1)

        @block.scalar
        def _(act):
            act.wait_ge(cs_neg, 2)
            act.activation(m.PCR, m.PCR, ACT.Exp, bias=m.RT[:, 0:1], scale=-1.0, accum_out=m.RT[:, 1:2])\
               .then_inc(ce_ready, 1)
            fetch(act, FETCHED[10:20])
            act.wait_ge(pt_ready, 1)
            act.activation(m.PCTT, m.PS[:, 1, 0:ROWS], ACT.Copy).then_inc(pt_read, 1)
            act.wait_ge(ss_neg, 1)
            act.activation(m.SL, m.SL, ACT.Exp, bias=m.RT[:, 6:7], scale=-1.0, accum_out=m.RT[:, 7:8])\
               .then_inc(se_ready, 1)
            act.wait_ge(pt_ready, 2)
            act.activation(m.PLT, m.PS[:, 4, :].rearrange("p (a b) -> p a b", b=ROWS), ACT.Copy).then_inc(pt_read, 1)

        @block.vector
        def _(dve):
            t = m.dve
            nsl = C[0:ROWS, C_NSL:C_NSL + 1]
            CB = m.BI.rearrange("p a b c -> p (a b c)")[:, 0:SBLK]
            t.chain(dve, dve.memset(m.KVG[(TOPK - 1) % 2 * DH:(TOPK - 1) % 2 * DH + DH, :, :, (TOPK - 1) // 2], 0.0))
            t.chain(dve, dve.tensor_scalar(CB, C[0:ROWS, C_CD:C_CD + SBLK], nsl, None, ALU.mult))
            dve.wait_ge(cs_ready, 1)
            dve.tensor_tensor_reduce(m.PCR, m.PS[0:ROWS, 0, 0:SBLK], CB, -1.0, 3e38, ALU.add, ALU.min, m.RT[:, 0:1])\
               .then_inc(cs_neg, 1)
            dve.wait_ge(ptj_in, 16)
            t.chain(dve, dve.tensor_copy(m.BAS, m.PTJ))
            dve.tensor_scalar(m.BAS, m.BAS, 2.0, C[:, C_PAR:C_PAR + 1], ALU.mult, ALU.add).then_inc(cs_neg, 1)
            dve.wait_ge(ce_ready, 1)
            t.chain(dve, dve.reciprocal(m.RT[:, 1:2], m.RT[:, 1:2]))
            dve.tensor_scalar(m.PCR, m.PCR, m.RT[:, 1:2], None, ALU.mult).then_inc(pc_ready, 1)
            dve.wait_ge(imp_sum, 1)
            dve.tensor_copy(m.IMP, m.PS[:, 1, 0:NBG16]).then_inc(imp_ready, 1)
            dve.wait_ge(imp_ready, 1)
            dve.memset(m.IMP[0:1], 1e30).then_inc(imp_ready, 1)
            dve.wait_ge(imp_rows, 1)
            dve.wait_ge(imp_ready, 2)
            for n in range(NBG16):
                row = m.PS[:, 4 + n // 4, n % 4 * P:(n % 4 + 1) * P]
                dve.scalar_tensor_tensor(out=m.EQ[:, 0], in0=row, scalar=m.IMP[:, n:n + 1],
                                         in1=C[:, C_TRI:C_TRI + P], op0=ALU.is_equal, op1=ALU.mult)\
                   .then_inc(rank_step, 1)
                dve.wait_ge(rank_step, 2 * n + 1)
                dve.scalar_tensor_tensor(out=m.EQ[:, 1], in0=row, scalar=m.IMP[:, n:n + 1], in1=m.EQ[:, 0],
                                         op0=ALU.is_gt, op1=ALU.add, accum_out=m.RK[:, n:n + 1]).then_inc(rank_step, 1)
                dve.wait_ge(rank_step, 2 * n + 2)
            t.chain(dve, dve.tensor_tensor(m.OHS.rearrange("p a b c -> p (a b) c"),
                                           m.RK.unsqueeze(2).to_broadcast([P, NBG16, TOPK]),
                                           C[:, C_S:C_S + TOPK].unsqueeze(1).to_broadcast([P, NBG16, TOPK]), ALU.is_equal))
            dve.tensor_tensor(m.WBJ[:, 0].rearrange("p a b c -> p a (b c)"), m.OHS.rearrange("p a b c -> p a (b c)"),
                              m.BAS.unsqueeze(2).to_broadcast([P, NB, G * TOPK]), ALU.mult).then_inc(wb_ready, 1)
            dve.tensor_scalar(m.WBJ[:, 1], m.OHS, C[:, C_J:C_J + 1], None, ALU.mult).then_inc(wb_ready, 1)
            dve.wait_ge(ids_ready, 1)
            dve.tensor_copy(m.IDX, m.PS[0:1, 2, 0:256]).then_inc(idx_ready, 1)
            t.chain(dve, dve.tensor_tensor(m.BRX, m.PS[0:ROWS, 3, 0:256].rearrange("p (a b) -> p a b", b=TOPK),
                                           C[0:ROWS, C_RM:C_RM + NBG16].unsqueeze(2).to_broadcast([ROWS, NBG16, TOPK]),
                                           ALU.mult))
            dve.tensor_reduce(m.BR, m.BRX.rearrange("p a b -> p b a"), AX_X, ALU.add).then_inc(idx_ready, 1)
            dve.wait_ge(idx_ready, 2)
            t.chain(dve, dve.tensor_scalar(m.BR, m.BR, -float(BLK), float(PAST), ALU.mult, ALU.add))
            for c in range(TOPK // 2):
                t.up(dve.tensor_tensor(m.BI[:, :, c], m.BR[:, 2 * c:2 * c + 2].unsqueeze(2).to_broadcast([ROWS, 2, BLK]),
                                       C[0:ROWS, C_L:C_L + BLK].unsqueeze(1).to_broadcast([ROWS, 2, BLK]), ALU.subtract))
            dve.wait_ge(t.sem, t.n)
            t.chain(dve, dve.tensor_scalar(m.BI, m.BI, nsl, None, ALU.mult))
            t.up(dve.memset(m.BI[:, 1, TOPK // 2 - 1], NEG))
            t.chain(dve, dve.tensor_scalar(m.SL[:, NK:NK + 1], m.RT[:, 4:5], -1.0, None, ALU.mult))
            dve.tensor_scalar(m.PCR, m.PCR, m.GS[:, 0:1], None, ALU.mult).then_inc(pg_ready, 1)
            dve.wait_ge(ss_ready, 1)
            t.chain(dve, dve.tensor_tensor_reduce(m.SL[:, 0:NK], m.PS[0:ROWS, 2:4].rearrange("p a b -> p (a b)"),
                                                  m.BI.rearrange("p a b c -> p (a b c)"), -1.0, 3e38, ALU.add, ALU.min,
                                                  m.RT[:, 2:3]))
            dve.tensor_tensor(m.RT[:, 6:7], m.RT[:, 2:3], m.SL[:, NK:NK + 1], ALU.min).then_inc(ss_neg, 1)
            dve.wait_ge(se_ready, 1)
            t.chain(dve, dve.reciprocal(m.RT[:, 7:8], m.RT[:, 7:8]))
            t.chain(dve, dve.tensor_tensor(m.RT[:, 7:8], m.RT[:, 7:8], m.GS[:, 1:2], ALU.mult))
            dve.tensor_scalar(m.BI.rearrange("p a b c -> p (a b c)").rearrange("p (c h l) -> p h c l", h=2, l=BLK),
                              m.SL[:, 0:NK].rearrange("p (h c l) -> p h c l", h=2, l=BLK), m.RT[:, 7:8], None,
                              ALU.mult).then_inc(ps_ready, 1)
            dve.tensor_scalar(m.DG, m.ident[0:ROWS, 0:ROWS], m.SL[:, NK:NK + 1], m.RT[:, 7:8], ALU.mult, ALU.mult)\
               .then_inc(ps_ready, 1)
            dve.wait_ge(o_ready, 1)
            v_new = m.SD[0:DH, :, 1].rearrange("p g b -> p b g").unsqueeze(3).to_broadcast([DH, NB, G, R])
            t.chain(dve, dve.tensor_tensor(m.TV.rearrange("p (b g r) -> p b g r", b=NB, g=G),
                                           m.PS[0:DH, 6, 0:ROWS].rearrange("p (b g r) -> p b g r", b=NB, g=G),
                                           v_new, ALU.mult))
            t.chain(dve, dve.tensor_tensor(m.TV, m.TV, m.OWT, ALU.add))
            dve.tensor_tensor(m.OT, m.TV, m.PS[0:DH, 5, 0:ROWS], ALU.add).then_inc(ot_ready, 1)
            dve.wait_ge(place_ready, 1)
            t.up(dve.tensor_copy(m.O[:, HEADS:HEADS + R, SEQ:TOK],
                                 m.PS[:, 7, 0:R * NB].rearrange("p (a b) -> p a b", b=NB)))


def program(nc, d):
    with ExitStack() as ctx:
        m = Memory()
        alloc(nc, ctx, m)
        with output_memory(nc, m, "layer0"):
            with mixer_memory(nc, m, "layer0"):
                attention_memory(m)
                sample_memory(m)
                norm(nc, m, 0, d)
                project_attention(nc, m, d)
                prepare_attention(nc, m, d)
                attention(nc, m, d)
                sample_window(nc, m, d)
                sample_compress(nc, m, d)
                sample_select(nc, m, d)
                lower_bounds(nc, m, d)
                linear_attention(nc, m, d, gla=False)
            add_projection(nc, m, "out_even", d["w_out_even"])
        ffn(nc, m, 1, d["w13_0"], d["w2_0"])
        with output_memory(nc, m, "layer1"):
            with mixer_memory(nc, m, "layer1"):
                norm(nc, m, 2)
                gate_factor(nc, m, d)
                linear_attention(nc, m, d, gla=True)
            add_projection(nc, m, "out_odd", d["w_out_odd"])
        ffn(nc, m, 3, d["w13_1"], d["w2_1"])
        with mixer_memory(nc, m, "last"):
            norm(nc, m, 4)
            store(nc, m, d)


def tiles(w, k=KT):
    n = w.shape[1] // P
    return np.ascontiguousarray(w.reshape(k, P, n, P).transpose(2, 1, 0, 3).reshape(n, P, k * P))


def pad_cols(w):
    return np.concatenate([w, np.zeros((w.shape[0], -w.shape[1] % P), w.dtype)], axis=1)


def constants(slopes):
    t = np.zeros((P, C_END), np.float32)
    row = np.arange(ROWS)
    j = np.arange(P)
    for g in range(G):
        t[g * DH + j % DH, C_SEL + g * P + j] = 1
        t[j[:DH], C_SHIFT + g * P + g * DH + j[:DH]] = 1
    t[row, C_RM + row // R] = 1
    t[row, C_NSL] = -slopes[row % (G * R)]
    for ch in range(24):
        t[ch, C_GM:C_GM + ROWS] = (row % R == ch % (G * R) // G) & (row // R % G == ch % G)
        t[ch, C_GJ + ch // (G * R)] = 1
    t[:, C_PAR], t[:, C_J] = j % 2, j
    t[:, C_TRI:C_TRI + P] = j[None, :] < j[:, None]
    t[:, C_S:C_S + TOPK] = np.arange(TOPK)
    t[:, C_L:C_L + BLK] = np.arange(BLK)
    t[:, C_CD:C_CD + SBLK] = PAST - BLK * j - (BLK - 1)
    return t


def layouts(x_prompt, x_sample, cache_nsa_kv, cache_win_kv, state_hgrn, state_gla, page_table,
            w_in_even, hg_lb_logits, hg_norm, nsa_cmp_pos, nsa_cmp_w1, nsa_cmp_w2, w_out_even,
            w_in_odd, gla_wa2, gla_ba, gla_norm, w_out_odd, norm_mix, norm_ffn, norm_final,
            ffn_w13, ffn_w2):
    a = {}
    x = np.concatenate([x_prompt[0], x_sample[:, 0]], axis=0)
    a["xT"] = x.T.reshape(KT, P, TOK).transpose(1, 0, 2)
    a["gains"] = np.stack([norm_mix[0], norm_ffn[0], norm_mix[1], norm_ffn[1], norm_final])\
        .reshape(5, KT, P).transpose(2, 0, 1)
    we = w_in_even[0]
    hg, at = we[:, :4 * 512], we[:, 4 * 512:]
    q = at[:, :512].reshape(DM, G, R, DH).transpose(0, 2, 1, 3).reshape(DM, 512)
    kv = at[:, 512:512 + 768]
    gates = pad_cols(at[:, 1280:].reshape(DM, G, R, 3).transpose(0, 3, 2, 1).reshape(DM, 24))
    heads = hg.reshape(DM, 4, HEADS, P).transpose(0, 2, 1, 3).reshape(DM, 2048)
    a["w_even"] = tiles(np.concatenate([q, kv, gates, heads], axis=1))
    wo = w_out_even[0]
    won = wo[512:].reshape(G, R, DH, DM).transpose(1, 0, 2, 3).reshape(512, DM)
    a["w_out_even"] = tiles(np.concatenate([wo[:512], won], axis=0))
    wd = w_in_odd[0]
    qk, v, a1, r = wd[:, :1024], wd[:, 1024:2048], wd[:, 2048:2064], wd[:, 2064:]
    perhead = np.concatenate([qk[:, :512].reshape(DM, HEADS, P), qk[:, 512:].reshape(DM, HEADS, P),
                              v.reshape(DM, HEADS, GV), r.reshape(DM, HEADS, GV)], axis=2).reshape(DM, -1)
    a["w_odd"] = tiles(np.concatenate([pad_cols(a1), perhead], axis=1))
    a["w_out_odd"] = tiles(w_out_odd[0])
    for l in range(2):
        w13 = ffn_w13[l].reshape(DM, 2, FT, P).transpose(0, 2, 1, 3).reshape(DM, 2 * FF)
        a[f"w13_{l}"] = tiles(w13)
        a[f"w2_{l}"] = tiles(ffn_w2[l], FT)
    a["lb"] = hg_lb_logits.reshape(2, HEADS, P).transpose(2, 0, 1)
    a["hg_gain"] = hg_norm[0].reshape(1, P).T
    a["gla_gain"] = gla_norm[0].reshape(2, P).T
    a["wa2"] = np.concatenate([gla_wa2[0], gla_ba[0][None]], axis=0)
    a["hg_in"] = state_hgrn[0].transpose(1, 2, 0, 3)[:, None]
    a["gla_in"] = state_gla[0].reshape(2, 4, HEADS, P, GV).transpose(2, 0, 3, 1, 4)
    w1 = nsa_cmp_w1[0].reshape(2, BLK, DH, DH)
    a["w1_dlh"] = w1.transpose(2, 0, 1, 3)
    a["w2_hd"] = nsa_cmp_w2[0].transpose(1, 0, 2)
    a["pe_dl"] = nsa_cmp_pos[0].transpose(2, 0, 1)
    slopes = 2.0 ** (-8.0 * np.arange(1, G * R + 1) / (G * R))
    a["nslope"] = np.broadcast_to(-slopes.reshape(G, R).T, (P, R, G)).astype(np.float32)
    a["w1_c"] = w1.reshape(2, BLK // 2, 2 * DH, DH).transpose(2, 0, 1, 3)
    a["pe_c"] = nsa_cmp_pos[0].reshape(2, BLK // 2, 2 * DH).transpose(2, 0, 1)
    pool = cache_nsa_kv[0].reshape(-1, 2, BLK, 4, G, DH)
    npool = pool.shape[0]
    a["cmp"] = pool[:, :, :, 0:2].reshape(npool, 2, BLK // 2, 2, 2, G, DH).transpose(0, 3, 6, 4, 2, 5, 1)\
        .reshape(npool, P, 256)
    k = pool[:, :, :, 2].transpose(0, 1, 3, 4, 2)
    v = pool[:, :, :, 3].transpose(0, 1, 3, 2, 4)
    a["slc"] = np.concatenate([k, v], axis=-1).reshape(npool * 2, G, BLK, P)
    a["pages"] = page_table.reshape(1, -1)
    a["block_page"] = np.repeat(page_table, 2, axis=1).T
    win = cache_win_kv[0]
    a["win_k"] = win[:, :, 0].reshape(NB, 2, WIN // 2, G, DH).transpose(1, 4, 0, 3, 2).reshape(P, NB * G, WIN // 2)
    a["win_v"] = win[:, :, 1].reshape(NB, WIN // P, P, G, DH).transpose(2, 0, 3, 1, 4)\
        .reshape(P, NB * G, WIN // P, DH)
    a["win_rows"] = win.reshape(NB, WIN, 2 * G * DH)
    a["win_dist"] = np.broadcast_to((WIN - np.arange(WIN)).astype(np.float32), (ROWS, WIN))
    a["table"] = constants(slopes)
    return {k: np.ascontiguousarray(v) for k, v in a.items()}


OUTS = {
    "yT": (P, KT, TOK), "kv_new": (P, TGATE - TKC, TOK), "win_kept": (NB, WIN - 1, 2 * G * DH),
    "hg_p": (HEADS, P, P), "hg_s": (HEADS, 1, P, NB, P), "gla_p": (HEADS, P, GV), "gla_s": (HEADS, 2, P, 4, GV),
}


def kernel(**inputs):
    import concourse.bacc as bacc
    from concourse.bass_utils import run_bass_kernel_spmd

    nc = bacc.Bacc("TRN2", target_bir_lowering=False, num_devices=1)
    arrays = {"in_" + k: v for k, v in layouts(**{k: np.asarray(v) for k, v in inputs.items()}).items()}
    d = {k[3:]: nc.dram_tensor(k, v.shape, mybir.dt.from_np(v.dtype), kind="ExternalInput").ap()
         for k, v in arrays.items()}
    for k, shape in OUTS.items():
        d[k] = nc.dram_tensor("out_" + k, shape, F32, kind="ExternalOutput").ap()
    program(nc, d)
    r = run_bass_kernel_spmd(nc, [arrays], core_ids=[0]).results[0]
    r = {k: np.asarray(r["out_" + k]) for k in OUTS}
    y = r["yT"].transpose(2, 1, 0).reshape(TOK, DM)
    kv = r["kv_new"].reshape(G, DH, 6, TOK).transpose(3, 2, 0, 1)
    win = np.concatenate([r["win_kept"].reshape(NB, WIN - 1, 2, G, DH), kv[SEQ:, None, 4:]], axis=1)
    hg_s = r["hg_s"].transpose(1, 3, 0, 2, 4).reshape(NB, HEADS, P, P)
    gla_s = r["gla_s"].transpose(1, 3, 0, 2, 4).reshape(NB, HEADS, P, GV)
    c = np.ascontiguousarray
    return (c(y[None, :SEQ]), c(y[SEQ:, None]), c(kv[None, None, :SEQ, :4]), c(kv[None, SEQ:, None, :4]),
            c(kv[None, None, SEQ - WIN:SEQ, 4:]), c(win[None]), c(r["hg_p"][None, None]), c(hg_s[None]),
            c(r["gla_p"][None, None]), c(gla_s[None]))
```
